# Optimizing a Trainium2 kernel written in Bass

```python
import jax, jax.numpy as jnp
from jax import lax
import numpy as np

D_MODEL = 1024
BATCH = 1
SEQ = 256
DEPTH = 2
DEC_BATCH = 8
DEC_SEQ = 8
PAST_LEN = 1024
PAGE_SIZE = 128

N_MIXERS = 2
N_SWA_LAYERS = (DEPTH + 1) // 2
N_GLA_LAYERS = DEPTH // 2

SWA_HEAD_DIM = 64
SWA_HEADS = D_MODEL // SWA_HEAD_DIM
SWA_KV_HEADS = SWA_HEADS // 4
SWA_GROUP = SWA_HEADS // SWA_KV_HEADS
WINDOW = 128
SWA_BLOCK = 128
ROPE_THETA = 10000.0

GLA_HEADS = 4
GLA_KEY_DIM = D_MODEL // 2
GLA_VAL_DIM = D_MODEL
GLA_DK = GLA_KEY_DIM // GLA_HEADS
GLA_DV = GLA_VAL_DIM // GLA_HEADS
GLA_GATE_RANK = 16
GLA_GATE_NORMALIZER = 16.0
GLA_CHUNK = 64

N_EXPERTS = 64
TOP_K = 8
N_GROUPS = 8
TOPK_GROUPS = 4
EXPERT_FF = D_MODEL // 4
SHARED_FF = EXPERT_FF
ROUTED_SCALE = 2.5
MOE_BLOCK = 128

NORM_EPS = 1e-6

kernel_name = "hybrid_swa_gla_moe_adaln_step"

def rms_norm(x, g):
    xf = x.astype(jnp.float32)
    y = xf * lax.rsqrt(jnp.mean(xf * xf, axis=-1, keepdims=True) + NORM_EPS)
    return (y * g.astype(jnp.float32)).astype(x.dtype)

def rope(x, pos):
    half = x.shape[-1] // 2
    inv = ROPE_THETA ** (-jnp.arange(half, dtype=jnp.float32) / half)
    ang = pos[:, None] * inv[None, :]
    cos = jnp.cos(ang)[:, None, :]
    sin = jnp.sin(ang)[:, None, :]
    xf = x.astype(jnp.float32)
    x1, x2 = xf[..., :half], xf[..., half:]
    return jnp.concatenate([x1 * cos - x2 * sin, x2 * cos + x1 * sin], axis=-1).astype(x.dtype)

def sink_softmax(scores, sink):
    s_col = jnp.broadcast_to(sink[..., None, None], scores.shape[:-1] + (1,))
    p = jax.nn.softmax(jnp.concatenate([scores, s_col], axis=-1), axis=-1)
    return p[..., :-1]

def swa_qkv(h, wqkv, pos):
    B, S, _ = h.shape
    qkv = h @ wqkv
    q, k, v = jnp.split(qkv, [SWA_HEADS * SWA_HEAD_DIM, (SWA_HEADS + SWA_KV_HEADS) * SWA_HEAD_DIM], axis=-1)
    q = rope(q.reshape(B, S, SWA_HEADS, SWA_HEAD_DIM), pos)
    k = rope(k.reshape(B, S, SWA_KV_HEADS, SWA_HEAD_DIM), pos)
    v = v.reshape(B, S, SWA_KV_HEADS, SWA_HEAD_DIM)
    return q, k, v

def swa_prompt(h, wqkv, sinks, wo):
    B, S, _ = h.shape
    q, k, v = swa_qkv(h, wqkv, jnp.arange(S, dtype=jnp.float32))
    nb = S // SWA_BLOCK
    qb = q.reshape(B, nb, SWA_BLOCK, SWA_KV_HEADS, SWA_GROUP, SWA_HEAD_DIM)

    def band(t):
        tb = t.reshape(B, nb, SWA_BLOCK, SWA_KV_HEADS, SWA_HEAD_DIM)
        prev = jnp.concatenate([jnp.zeros_like(tb[:, :1]), tb[:, :-1]], axis=1)
        return jnp.concatenate([prev, tb], axis=2)

    kb, vb = band(k), band(v)
    scores = jnp.einsum('bnqkgd,bnskd->bnkgqs', qb, kb).astype(jnp.float32) * (SWA_HEAD_DIM ** -0.5)
    qi = jnp.arange(SWA_BLOCK)[:, None]
    sj = jnp.arange(2 * SWA_BLOCK)[None, :]
    rel = qi + SWA_BLOCK - sj
    key_pos = jnp.arange(nb)[:, None, None] * SWA_BLOCK + sj - SWA_BLOCK
    mask = (rel >= 0) & (rel <= WINDOW) & (key_pos >= 0)
    scores = jnp.where(mask[None, :, None, None], scores, -jnp.inf)
    p = sink_softmax(scores, sinks.reshape(SWA_KV_HEADS, SWA_GROUP).astype(jnp.float32)).astype(v.dtype)
    o = jnp.einsum('bnkgqs,bnskd->bnqkgd', p, vb).reshape(B, S, SWA_HEADS * SWA_HEAD_DIM)
    return o @ wo, k[:, S - WINDOW:], v[:, S - WINDOW:]

def swa_sample(h, k_buf, v_buf, wqkv, sinks, wo):
    B, T, _ = h.shape
    q, k, v = swa_qkv(h, wqkv, PAST_LEN + jnp.arange(T, dtype=jnp.float32))
    keys = jnp.concatenate([k_buf.astype(k.dtype), k], axis=1)
    vals = jnp.concatenate([v_buf.astype(v.dtype), v], axis=1)
    qg = q.reshape(B, T, SWA_KV_HEADS, SWA_GROUP, SWA_HEAD_DIM)
    scores = jnp.einsum('btkgd,bskd->bkgts', qg, keys).astype(jnp.float32) * (SWA_HEAD_DIM ** -0.5)
    q_pos = PAST_LEN + jnp.arange(T)[:, None]
    k_pos = PAST_LEN - WINDOW + jnp.arange(WINDOW + T)[None, :]
    rel = q_pos - k_pos
    mask = (rel >= 0) & (rel <= WINDOW) & (k_pos >= 0)
    scores = jnp.where(mask, scores, -jnp.inf)
    p = sink_softmax(scores, sinks.reshape(SWA_KV_HEADS, SWA_GROUP).astype(jnp.float32)).astype(vals.dtype)
    o = jnp.einsum('bkgts,bskd->btkgd', p, vals).reshape(B, T, SWA_HEADS * SWA_HEAD_DIM)
    return o @ wo, keys[:, -WINDOW:], vals[:, -WINDOW:]

def gla_project(h, win, wa1, wa2, ba):
    B, S, _ = h.shape
    proj = h @ win
    q, k, v, r = jnp.split(proj, [GLA_KEY_DIM, 2 * GLA_KEY_DIM, 2 * GLA_KEY_DIM + GLA_VAL_DIM], axis=-1)
    gate_logit = (h @ wa1) @ wa2 + ba
    g = jax.nn.log_sigmoid(gate_logit.astype(jnp.float32)) / GLA_GATE_NORMALIZER

    def heads(t, d):
        return jnp.moveaxis(t.astype(jnp.float32).reshape(B, S, GLA_HEADS, d), 2, 1)

    return heads(q, GLA_DK) * (GLA_DK ** -0.5), heads(k, GLA_DK), heads(v, GLA_DV), heads(g, GLA_DK), r

def gla_chunk(s0, qkvg):
    q, k, v, g = qkvg
    L = q.shape[2]
    b = jnp.cumsum(g, axis=2)
    o_inter = jnp.einsum('bhtd,bhde->bhte', q * jnp.exp(b), s0)
    causal = jnp.tril(jnp.ones((L, L), dtype=bool))[:, :, None]
    diff = b[:, :, :, None, :] - b[:, :, None, :, :]
    decay = jnp.exp(jnp.where(causal, diff, -jnp.inf))
    attn = jnp.sum(q[:, :, :, None, :] * k[:, :, None, :, :] * decay, axis=-1)
    o = o_inter + jnp.einsum('bhts,bhse->bhte', attn, v)
    b_last = b[:, :, -1]
    s_new = jnp.exp(b_last)[..., None] * s0 + jnp.einsum('bhsd,bhse->bhde', k * jnp.exp(b_last[:, :, None] - b), v)
    return s_new, o

def gla_output(o, r, norm_g, wo, dtype):
    B, H, S, _ = o.shape
    o = rms_norm(o, norm_g)
    o = jnp.moveaxis(o, 1, 2).reshape(B, S, GLA_VAL_DIM)
    return (o * jax.nn.silu(r.astype(jnp.float32))).astype(dtype) @ wo

def gla_prompt(h, win, wa1, wa2, ba, norm_g, wo):
    B, S, _ = h.shape
    q, k, v, g, r = gla_project(h, win, wa1, wa2, ba)
    nc = S // GLA_CHUNK

    def chunks(t):
        return jnp.moveaxis(t.reshape(B, GLA_HEADS, nc, GLA_CHUNK, t.shape[-1]), 2, 0)

    s0 = jnp.zeros((B, GLA_HEADS, GLA_DK, GLA_DV), jnp.float32)
    s_final, o = lax.scan(gla_chunk, s0, (chunks(q), chunks(k), chunks(v), chunks(g)))
    o = jnp.moveaxis(o, 0, 2).reshape(B, GLA_HEADS, S, GLA_DV)
    return gla_output(o, r, norm_g, wo, h.dtype), s_final.astype(h.dtype)

def gla_sample(h, state, win, wa1, wa2, ba, norm_g, wo):
    q, k, v, g, r = gla_project(h, win, wa1, wa2, ba)
    s_new, o = gla_chunk(state.astype(jnp.float32), (q, k, v, g))
    return gla_output(o, r, norm_g, wo, h.dtype), s_new.astype(state.dtype)

def routed_experts(x, eidx, gate, wg, wu, wd):
    T, D = x.shape
    n_assign = T * TOP_K
    n_blocks = -(-n_assign // MOE_BLOCK) + N_EXPERTS
    e_flat = eidx.reshape(-1)
    tok_flat = jnp.repeat(jnp.arange(T, dtype=jnp.int32), TOP_K)
    order = jnp.argsort(e_flat)
    e_sorted = e_flat[order]
    counts = jnp.bincount(e_flat, length=N_EXPERTS)
    padded = (counts + MOE_BLOCK - 1) // MOE_BLOCK * MOE_BLOCK
    pad_end = jnp.cumsum(padded)
    pad_start = pad_end - padded
    start = jnp.cumsum(counts) - counts
    dest = pad_start[e_sorted] + jnp.arange(n_assign) - start[e_sorted]
    slot_tok = jnp.full((n_blocks * MOE_BLOCK,), T, jnp.int32).at[dest].set(tok_flat[order])
    slot_w = jnp.zeros((n_blocks * MOE_BLOCK,), gate.dtype).at[dest].set(gate.reshape(-1)[order])
    block_e = jnp.minimum(jnp.searchsorted(pad_end, jnp.arange(n_blocks) * MOE_BLOCK, side='right'), N_EXPERTS - 1)
    x_pad = jnp.concatenate([x, jnp.zeros((1, D), x.dtype)], axis=0)

    def one_block(args):
        tok, w, e = args
        xb = x_pad[tok]
        hb = jax.nn.silu(xb @ wg[e]) * (xb @ wu[e])
        return (hb @ wd[e]) * w[:, None]

    yb = lax.map(one_block, (slot_tok.reshape(n_blocks, MOE_BLOCK), slot_w.reshape(n_blocks, MOE_BLOCK), block_e))
    return jnp.zeros((T + 1, D), x.dtype).at[slot_tok].add(yb.reshape(-1, D))[:T]

def moe(h, router_w, router_b, wg, wu, wd, swg, swu, swd):
    B, S, D = h.shape
    x = h.reshape(-1, D)
    T = x.shape[0]
    scores = jax.nn.sigmoid((x @ router_w).astype(jnp.float32))
    sel = scores + router_b.astype(jnp.float32)
    grp_score = jnp.sum(lax.top_k(sel.reshape(T, N_GROUPS, -1), 2)[0], axis=-1)
    _, gidx = lax.top_k(grp_score, TOPK_GROUPS)
    gmask = jnp.any(gidx[:, :, None] == jnp.arange(N_GROUPS)[None, None, :], axis=1)
    emask = jnp.repeat(gmask, N_EXPERTS // N_GROUPS, axis=1)
    _, eidx = lax.top_k(jnp.where(emask, sel, -jnp.inf), TOP_K)
    w = jnp.take_along_axis(scores, eidx, axis=1)
    w = w / jnp.sum(w, axis=-1, keepdims=True) * ROUTED_SCALE
    routed = routed_experts(x, eidx, w.astype(x.dtype), wg, wu, wd)
    shared = (jax.nn.silu(x @ swg) * (x @ swu)) @ swd
    return (routed + shared).reshape(B, S, D)

def setup_inputs(seed: int = 0) -> dict:
    key = jax.random.key(seed)
    ks = iter(jax.random.split(key, 40))
    f32 = jnp.float32

    def nrm(shape, scale):
        return jax.random.normal(next(ks), shape, f32) * scale

    D = D_MODEL
    qkv_w = (SWA_HEADS + 2 * SWA_KV_HEADS) * SWA_HEAD_DIM
    gla_in = 2 * GLA_KEY_DIM + 2 * GLA_VAL_DIM
    return {
        "x_prompt": nrm((BATCH, SEQ, D), 1.0),
        "x_sample": nrm((DEC_BATCH, DEC_SEQ, D), 1.0),
        "c_prompt": nrm((BATCH, D), 1.0),
        "c_sample": nrm((DEC_BATCH, D), 1.0),
        "cache_swa_k": nrm((N_SWA_LAYERS, DEC_BATCH, WINDOW, SWA_KV_HEADS, SWA_HEAD_DIM), 1.0),
        "cache_swa_v": nrm((N_SWA_LAYERS, DEC_BATCH, WINDOW, SWA_KV_HEADS, SWA_HEAD_DIM), 1.0),
        "state_gla": nrm((N_GLA_LAYERS, DEC_BATCH, GLA_HEADS, GLA_DK, GLA_DV), 0.5),
        "norm_mix_g": 1.0 + nrm((DEPTH, D), 0.05),
        "norm_ffn_g": 1.0 + nrm((DEPTH, D), 0.05),
        "final_g": 1.0 + nrm((D,), 0.05),
        "ada_w": nrm((DEPTH, D, 6 * D), 0.5 * D ** -0.5),
        "ada_b": nrm((DEPTH, 6 * D), 0.02),
        "swa_wqkv": nrm((N_SWA_LAYERS, D, qkv_w), D ** -0.5),
        "swa_sinks": nrm((N_SWA_LAYERS, SWA_HEADS), 0.5),
        "swa_wo": nrm((N_SWA_LAYERS, SWA_HEADS * SWA_HEAD_DIM, D), (SWA_HEADS * SWA_HEAD_DIM) ** -0.5),
        "gla_win": nrm((N_GLA_LAYERS, D, gla_in), D ** -0.5),
        "gla_wa1": nrm((N_GLA_LAYERS, D, GLA_GATE_RANK), D ** -0.5),
        "gla_wa2": nrm((N_GLA_LAYERS, GLA_GATE_RANK, GLA_KEY_DIM), GLA_GATE_RANK ** -0.5),
        "gla_ba": nrm((N_GLA_LAYERS, GLA_KEY_DIM), 0.1),
        "gla_norm_g": 1.0 + nrm((N_GLA_LAYERS, GLA_DV), 0.05),
        "gla_wo": nrm((N_GLA_LAYERS, GLA_VAL_DIM, D), GLA_VAL_DIM ** -0.5),
        "moe_router": nrm((DEPTH, D, N_EXPERTS), D ** -0.5),
        "moe_bias": nrm((DEPTH, N_EXPERTS), 0.01),
        "moe_wg": nrm((DEPTH, N_EXPERTS, D, EXPERT_FF), D ** -0.5),
        "moe_wu": nrm((DEPTH, N_EXPERTS, D, EXPERT_FF), D ** -0.5),
        "moe_wd": nrm((DEPTH, N_EXPERTS, EXPERT_FF, D), EXPERT_FF ** -0.5),
        "shared_wg": nrm((DEPTH, D, SHARED_FF), D ** -0.5),
        "shared_wu": nrm((DEPTH, D, SHARED_FF), D ** -0.5),
        "shared_wd": nrm((DEPTH, SHARED_FF, D), SHARED_FF ** -0.5),
    }

def reference(x_prompt, x_sample, c_prompt, c_sample, cache_swa_k, cache_swa_v, state_gla,
              norm_mix_g, norm_ffn_g, final_g, ada_w, ada_b,
              swa_wqkv, swa_sinks, swa_wo,
              gla_win, gla_wa1, gla_wa2, gla_ba, gla_norm_g, gla_wo,
              moe_router, moe_bias, moe_wg, moe_wu, moe_wd,
              shared_wg, shared_wu, shared_wd):

    def run(x, c, swa_k, swa_v, gla_s):
        sample = swa_k is not None
        new_k, new_v, new_s = [], [], []
        for layer in range(DEPTH):
            mod = (jax.nn.silu(c) @ ada_w[layer] + ada_b[layer])[:, None, :]
            sh1, sc1, g1, sh2, sc2, g2 = jnp.split(mod, 6, axis=-1)
            hmix = rms_norm(x, norm_mix_g[layer]) * (1.0 + sc1) + sh1
            if layer % N_MIXERS == 0:
                a = layer // N_MIXERS
                if sample:
                    out, kk, vv = swa_sample(hmix, swa_k[a], swa_v[a], swa_wqkv[a], swa_sinks[a], swa_wo[a])
                else:
                    out, kk, vv = swa_prompt(hmix, swa_wqkv[a], swa_sinks[a], swa_wo[a])
                new_k.append(kk)
                new_v.append(vv)
            else:
                m = layer // N_MIXERS
                if sample:
                    out, ss = gla_sample(hmix, gla_s[m], gla_win[m], gla_wa1[m], gla_wa2[m], gla_ba[m], gla_norm_g[m], gla_wo[m])
                else:
                    out, ss = gla_prompt(hmix, gla_win[m], gla_wa1[m], gla_wa2[m], gla_ba[m], gla_norm_g[m], gla_wo[m])
                new_s.append(ss)
            x = x + g1 * out
            hffn = rms_norm(x, norm_ffn_g[layer]) * (1.0 + sc2) + sh2
            x = x + g2 * moe(hffn, moe_router[layer], moe_bias[layer], moe_wg[layer], moe_wu[layer],
                             moe_wd[layer], shared_wg[layer], shared_wu[layer], shared_wd[layer])
        return rms_norm(x, final_g), jnp.stack(new_k), jnp.stack(new_v), jnp.stack(new_s)

    y_prompt, swa_k_prompt, swa_v_prompt, gla_state_prompt = run(x_prompt, c_prompt, None, None, None)
    y_sample, swa_k_sample, swa_v_sample, gla_state_sample = run(x_sample, c_sample, cache_swa_k, cache_swa_v, state_gla)
    return (y_prompt, y_sample, swa_k_prompt, swa_v_prompt, swa_k_sample, swa_v_sample, gla_state_prompt, gla_state_sample)


_drawn_inputs = setup_inputs


def setup_inputs(seed=0):
    import zlib

    import numpy as np

    out = dict(_drawn_inputs(seed))
    spreads = {}
    factors = {'swa_sinks': 7.515}
    for name, (base, spread) in spreads.items():
        noise = np.random.default_rng([zlib.crc32(name.encode()), seed]).standard_normal(out[name].shape)
        drawn = base * np.exp(spread * noise) if base else spread * noise
        out[name] = __import__('jax').numpy.asarray(drawn.astype(out[name].dtype))
    for name, factor in factors.items():
        out[name] = (out[name] * factor).astype(out[name].dtype)
    return out
```

```python
from contextlib import ExitStack

import concourse.bass as bass
import numpy as np
from concourse import mybir

F32 = mybir.dt.float32
F32R = mybir.dt.float32r
BF16 = mybir.dt.bfloat16
I32 = mybir.dt.int32
ALU = mybir.AluOpType
ACT = mybir.ActivationFunctionType
AX = mybir.AxisListType

P = 128
D = 1024
KC = D // P
SEQ = 256
DB, DT = 8, 8
NS = DB * DT
T = SEQ + NS
TILES = [(0, 128), (128, 128), (256, 64)]
NC_ = 1 + DB
WIN = 128
HEADS, KVH, HD = 16, 4, 64
G = HEADS // KVH
GH, DK, DV = 4, 128, 256
NE, FF = 64, 256
CAP = 64
NGRP = 8
EPS = 1e-6
BIG = 1000.0
NEG = -1e30
SLOT = 6144
GUW = 4096

V1_ADAB = 0
V2_MIX, V2_FFN, V2_FIN, V2_BA, V2_GN, V2_CP, V2_CS, V2_N = 0, 16, 32, 40, 44, 46, 54, 118


CONSTS = dict(
    all=dict(ident=128, ones=128, slot=64, tie=64),
    start=dict(upper=128, upper2=128),
    swa=dict(cos=96, sin=96, mask0=128, mask1=256, maskc=128, maskn=120),
    gla=dict(tri=128, tri8=64, reset=320, rowsel=8),
)


def const_layout():
    at, out, ranges = 0, {}, {}
    for part, sizes in CONSTS.items():
        lo = at
        for k, n in sizes.items():
            out[k] = (at, n)
            at += n
        ranges[part] = (lo, at)
    return out, ranges, at


def const_table():
    lay, _, n = const_layout()
    c = np.zeros((P, n), np.float32)

    def put(name, a):
        a = np.asarray(a, np.float32).reshape(a.shape[0], -1)
        c[:a.shape[0], lay[name][0]:lay[name][0] + a.shape[1]] = a

    i, j = np.arange(P)[:, None], np.arange(P)[None, :]
    put("ident", i == j)
    put("ones", np.ones((P, P)))
    put("upper", i < j)
    put("upper2", i[:64] < j % 64)
    put("slot", np.broadcast_to(np.arange(CAP), (P, CAP)))
    half = HD // 2
    inv = (np.float32(10000.0) ** (-np.arange(half, dtype=np.float32) / np.float32(half))).astype(np.float32)
    pos = np.zeros((3, P), np.float32)
    pos[0], pos[1] = np.arange(P), P + np.arange(P)
    pos[2, :NS] = 1024 + np.arange(NS) % DT
    ang = (pos[:, :, None] * inv[None, None, :]).astype(np.float32)
    put("cos", np.cos(ang).transpose(1, 0, 2))
    put("sin", np.sin(ang).transpose(1, 0, 2))
    put("mask0", np.where(j <= i, 0.0, NEG))
    s = np.arange(2 * P)[None, :]
    rel = i + P - s
    put("mask1", np.where((rel >= 0) & (rel <= WIN), 0.0, NEG))
    t = i % DT
    put("maskc", np.where(j >= t, 0.0, NEG))
    w = np.arange(120)[None, :] - 56
    put("maskn", np.where((w >= 0) & (w <= t), 0.0, NEG))
    put("tri", i <= j)
    a, b = np.arange(NS)[:, None], np.arange(NS)[None, :]
    put("tri8", (a // DT == b // DT) & (a <= b))
    tok = np.arange(T)
    put("reset", np.broadcast_to(np.where((tok == 0) | (tok == P) | ((tok >= SEQ) & (tok % DT == 0)), 0.0, 1.0), (P, T)))
    put("rowsel", a // DT == np.arange(DB)[None, :])
    put("tie", np.broadcast_to((np.arange(8)[None, :] < np.arange(8)[:, None]).reshape(1, 64), (P, 64)))
    return c


class Flag:

    def __init__(self, handle):
        self.h, self.n = handle, 0

    def up(self, ins, k=1):
        ins.then_inc(self.h, k)
        self.n += k
        return self.n

    def wait(self, eng, n=None):
        n = self.n if n is None else n
        if n > 0:
            eng.wait_ge(self.h, n)


def decoder_step(nc, a, debug=None):
    with ExitStack() as ctx:
        names = {}

        def sb(name, shape, dt=F32, c=ctx):
            names[name] = names.get(name, -1) + 1
            return c.enter_context(nc.sbuf_tensor(f"s_{name}_{names[name]}", shape, dt))

        def sem(name):
            return ctx.enter_context(nc.semaphore(name))

        def flag(name):
            return Flag(sem(name))

        pair = [ctx.enter_context(nc.psum_tensor(f"banks{i}", [P, 2, 512], F32)) for i in range(2)]
        bank = [pair[i // 2][:, i % 2, :] for i in range(4)]
        ybank = ctx.enter_context(nc.psum_tensor("ybank", [P, 2, 512], F32))
        bank += [ybank[:, 0, :], ybank[:, 1, :]]
        bank += [ctx.enter_context(nc.psum_tensor(f"bank{i}", [P, 512], F32)) for i in (6, 7)]

        ring = sb("ring", [P, 4, SLOT])
        xT = sb("xT", [P, KC, T])
        hT = sb("hT", [P, KC, T])
        mod = [sb(f"mod{i}", [P, 48, NC_]) for i in range(2)]
        lay, const_range, _ = const_layout()
        csts = {"all": sb("cst", [P, const_range["all"][1]])}
        vt1 = sb("vt1", [P, 96])
        vt2 = sb("vt2", [P, V2_N])
        condT = sb("condT", [P, KC, 32])
        upper_b = sb("upper_b", [P, 3, P], BF16)
        biasr = sb("biasr", [P, 2, NE])
        router = sb("router", [P, KC, NE])
        rstd = sb("rstd", [P, T])

        def cc(name):
            at, n = lay[name]
            part = next(p for p, (lo, hi) in const_range.items() if lo <= at < hi)
            lo = const_range[part][0]
            return csts[part][:, at - lo:at - lo + n]

        def const_load(part, c):
            lo, hi = const_range[part]
            if part not in csts:
                csts[part] = sb("cst_" + part, [P, hi - lo], c=c)

            @block.gpsimd
            def _(pool):
                aux_in.up(pool.dma_start(csts[part][:, :], a["consts"][:, lo:hi]), 16)

        ident, ones = cc("ident"), cc("ones")

        pe_done, act_done, dve_done, aux_in, stored = (flag(n) for n in ("pe_done", "act_done", "dve_done", "aux_in", "stored"))
        phase = flag("phase_done")
        slot_in = [flag(f"gu_in{s}") for s in range(4)]
        down_in = [flag(f"down_in{s}") for s in range(4)]
        item_used = flag("item_used")
        last_item = [None] * 4

        block = ctx.enter_context(nc.Block())

        def barrier():
            n = phase.n + 4

            def meet(eng):
                phase.up(eng.drain())
                eng.wait_ge(phase.h, n)

            @block.tensor
            def _(pe):
                meet(pe)

            @block.scalar
            def _(act):
                meet(act)

            @block.vector
            def _(dve):
                meet(dve)

            @block.gpsimd
            def _(pool):
                stored.wait(pool)
                meet(pool)

        items = [0]

        def stream(slot, parts):
            @block.sync
            def _(sp):
                if last_item[slot]:
                    sp.wait_ge(*last_item[slot])
                for dst, src in parts(ring[:, slot, 0:GUW].rearrange("p (k n) -> p k n", n=512)):
                    slot_in[slot].up(sp.dma_start(dst, src), 16)
            items[0] += 1
            last_item[slot] = (item_used.h, items[0])

        def columns(w, c0):
            return lambda dst: [(dst, w[:, c0:c0 + 512].rearrange("(k p) n -> p k n", p=P))]

        def item(slot):
            return ring[:, slot, 0:GUW].rearrange("p (k n) -> p k n", n=512)

        def start():
            c0 = ExitStack()
            v1 = sb("v1", [96, P], c=c0)
            v2 = sb("v2", [V2_N, P], c=c0)
            xtok = sb("xtok", [P, 3, D], c=c0)

            const_load("all", c0)
            const_load("start", c0)

            @block.gpsimd
            def _(pool):
                def load(dst, src):
                    aux_in.up(pool.dma_start(dst, src), 16)

                load(v2[V2_CP:V2_CP + 8, :], a["c_prompt"].rearrange("a (k p) -> (a k) p", p=P))
                load(v2[V2_CS:V2_CS + 64, :], a["c_sample"].rearrange("a (k p) -> (a k) p", p=P))
                load(v1[:, :], a["ada_b"].rearrange("l (k p) -> (l k) p", p=P))
                load(v2[V2_MIX:V2_MIX + 16, :], a["norm_mix_g"].rearrange("l (k p) -> (l k) p", p=P))
                load(v2[V2_FFN:V2_FFN + 16, :], a["norm_ffn_g"].rearrange("l (k p) -> (l k) p", p=P))
                load(v2[V2_FIN:V2_FIN + 8, :], a["final_g"].rearrange("(k p) -> k p", p=P))
                load(v2[V2_BA:V2_BA + 4, :], a["gla_ba"].rearrange("l (k p) -> (l k) p", p=P))
                load(v2[V2_GN:V2_GN + 2, :], a["gla_norm_g"].rearrange("l (k p) -> (l k) p", p=P))
                load(xtok[:, 0:2, :], a["x_prompt"][0].rearrange("(t p) d -> p t d", p=P))
                load(xtok[0:NS, 2, :], a["x_sample"].rearrange("b t d -> (b t) d"))
                load(biasr[:, :, :], a["moe_bias"].rearrange("(o l) e -> o l e", o=1).to_broadcast([P, 2, NE]))

            @block.vector
            def _(dve):
                dve_done.up(dve.memset(condT[:, :, :], 0.0))

            @block.tensor
            def _(pe):
                aux_in.wait(pe)
                pe.transpose(bank[0][:, 0:96], v1[:, :], ident[0:96, 0:96])
                pe_done.up(pe.transpose(bank[1][:, 0:V2_N], v2[:, :], ident[0:V2_N, 0:V2_N]))

            @block.vector
            def _(dve):
                aux_in.wait(dve)
                pe_done.wait(dve)
                dve.tensor_copy(vt1[:, :], bank[0][:, 0:96])
                dve.tensor_copy(vt2[:, :], bank[1][:, 0:V2_N])
                dve.tensor_copy(upper_b[:, 0, :], cc("upper"))
                dve.tensor_copy(upper_b[:, 1, :], cc("upper2"))
                dve_done.up(dve.tensor_copy(upper_b[:, 2, :], ones))

            @block.scalar
            def _(act):
                dve_done.wait(act)
                act.activation(condT[:, :, 0], vt2[:, V2_CP:V2_CP + 8], ACT.Silu)
                act_done.up(act.activation(condT[:, :, 1:NC_], vt2[:, V2_CS:V2_CS + 64].rearrange("p (b k) -> p k b", k=KC),
                                           ACT.Silu))

            def to_features(eng_name, src, dst, base):
                for n, (t, k4) in enumerate((t, k4) for t in range(3) for k4 in range(2)):
                    b = bank[2 + n % 4]
                    t0, tn = TILES[t]
                    who = (act_done, dve_done)[n % 2]

                    @block.tensor
                    def _(pe):
                        if n >= 4:
                            pe.wait_ge(who.h, base[n % 2][n - 4])
                        for j in range(4):
                            k = 4 * k4 + j
                            last = pe.transpose(b[:, j * P:j * P + tn], src(t, k), ident[0:tn, 0:tn])
                        pe_done.up(last)

                    o, i = dst[:, 4 * k4:4 * k4 + 4, t0:t0 + tn], b.rearrange("p (j t) -> p j t", t=P)[:, :, 0:tn]
                    if n % 2 == 0:
                        @block.scalar
                        def _(act):
                            pe_done.wait(act)
                            act_done.up(act.copy(o, i))
                    else:
                        @block.vector
                        def _(dve):
                            pe_done.wait(dve)
                            dve_done.up(dve.tensor_copy(o, i))
                    base[n % 2][n] = who.n

            to_features("x", lambda t, k: xtok[0:TILES[t][1], t, k * P:(k + 1) * P], xT, [{}, {}])
            barrier()
            c0.close()

        def ada_round(l, r, ada_sb):
            slot = ada_slots[(l, r)]

            @block.tensor
            def _(pe):
                slot_in[slot].wait(pe, ada_in[(l, r)])
                act_done.wait(pe)
                w = item(slot)
                for k in range(KC):
                    for j in range(4):
                        last = pe.matmul(bank[6][32 * j:32 * j + 32, 0:P], condT[:, k, :], w[:, k, j * P:(j + 1) * P],
                                         start=(k == 0), stop=(k == KC - 1))
                item_used.up(last)
            used = item_used.n

            @block.scalar
            def _(act):
                act.wait_ge(item_used.h, used)
                pe_done.wait(act)
                act_done.up(act.copy(ada_sb[:, :], bank[6][:, 0:P]))

            @block.tensor
            def _(pe):
                act_done.wait(pe)
                dve_done.wait(pe)
                pe_done.up(pe.transpose(bank[7][:, 0:P], ada_sb[:, :], ident))

            @block.vector
            def _(dve):
                pe_done.wait(dve)
                dve_done.up(dve.tensor_tensor(
                    mod[l][:, 4 * r:4 * r + 4, :], bank[7][:, 0:P].rearrange("p (j c) -> p j c", c=32)[:, :, 0:NC_],
                    vt1[:, 48 * l + 4 * r:48 * l + 4 * r + 4].unsqueeze(2).to_broadcast([P, 4, NC_]), ALU.add))

        ada_slots, ada_in = {}, {}

        def ada_stream(l, r, slot):
            ada_slots[(l, r)] = slot
            stream(slot, columns(a["ada_w"][l], 512 * r))
            ada_in[(l, r)] = slot_in[slot].n

        def ada_finish(l):
            @block.vector
            def _(dve):
                dve_done.wait(dve)
                for sec, row in ((1, V2_MIX + 8 * l), (4, V2_FFN + 8 * l)):
                    s = mod[l][:, 8 * sec:8 * sec + 8, :]
                    dve_done.up(dve.scalar_tensor_tensor(
                        s, s, 1.0, vt2[:, row:row + 8].unsqueeze(2).to_broadcast([P, KC, NC_]), ALU.add, ALU.mult))

        def bc_t(ap, n=KC):
            return ap.unsqueeze(3).to_broadcast([P, n, DB, DT])

        def sample_view(ap):
            return ap[:, :, SEQ:T].rearrange("p k (b t) -> p k b t", t=DT)

        def norm(scale, shift):
            @block.scalar
            def _(act):
                dve_done.wait(act)
                act_done.up(act.activation(hT[:, 0:4, :], xT[:, 0:4, :], ACT.Square))

            @block.vector
            def _(dve):
                dve_done.wait(dve)
                dve_done.up(dve.tensor_tensor(hT[:, 4:8, :], xT[:, 4:8, :], xT[:, 4:8, :], ALU.mult))

            @block.tensor
            def _(pe):
                act_done.wait(pe)
                dve_done.wait(pe)
                for k in range(KC):
                    last = pe.matmul(bank[0][:, 0:T], ones, hT[:, k, :], start=(k == 0), stop=(k == KC - 1))
                pe_done.up(last)

            @block.vector
            def _(dve):
                pe_done.wait(dve)
                dve_done.up(dve.tensor_scalar(rstd[:, :], bank[0][:, 0:T], 1.0 / D, EPS, ALU.mult, ALU.add))
                dve_done.wait(dve)
                dve_done.up(dve.reciprocal(rstd[:, :], rstd[:, :]))

            @block.scalar
            def _(act):
                dve_done.wait(act)
                act_done.up(act.activation(rstd[:, :], rstd[:, :], ACT.Sqrt))

            @block.vector
            def _(dve):
                act_done.wait(dve)
                dve_done.up(dve.tensor_tensor(hT[:, :, :], xT[:, :, :], rstd[:, :].unsqueeze(1).to_broadcast([P, KC, T]), ALU.mult))
                dve_done.wait(dve)
                if shift is not None:
                    s = sample_view(hT)
                    dve_done.up(dve.tensor_tensor(s, s, bc_t(scale[:, :, 1:NC_]), ALU.mult))
                    dve_done.wait(dve)
                    dve_done.up(dve.tensor_tensor(s, s, bc_t(shift[:, :, 1:NC_]), ALU.add))

            @block.scalar
            def _(act):
                dve_done.wait(act)
                for k in range(KC):
                    if shift is not None:
                        h = hT[:, k, 0:SEQ]
                        last = act.activation(h, h, ACT.Identity, scale=scale[:, k, 0:1], bias=shift[:, k, 0:1])
                    else:
                        last = act.activation(hT[:, k, :], hT[:, k, :], ACT.Copy, scale=scale[:, k:k + 1])
                act_done.up(last)

        def gated_add(dve, m, src, gate, tmp):
            dve_done.wait(dve)
            dve.scalar_tensor_tensor(xT[:, m, 0:SEQ], src[:, 0:SEQ], gate[:, m, 0:1], xT[:, m, 0:SEQ], ALU.mult, ALU.add)
            tv = tmp.rearrange("p (b t) -> p b t", t=DT)
            dve_done.up(dve.tensor_tensor(tv, src[:, SEQ:T].rearrange("p (b t) -> p b t", t=DT),
                                          gate[:, m, 1:NC_].unsqueeze(2).to_broadcast([P, DB, DT]), ALU.mult))
            dve_done.wait(dve)
            dve_done.up(dve.tensor_tensor(xT[:, m, SEQ:T], xT[:, m, SEQ:T], tmp[:, :], ALU.add))

        def out_projection(slots, src, gate, tmp):
            freed = {}
            for m in range(KC):
                (slot, seen_in), b = slots[m // 4], bank[m % 2]
                w = item(slot)

                @block.tensor
                def _(pe):
                    if m % 4 == 0:
                        slot_in[slot].wait(pe, seen_in)
                    if m >= 2:
                        pe.wait_ge(dve_done.h, freed[m - 2])
                    for k in range(KC):
                        last = pe.matmul(b[:, 0:T], w[:, k, (m % 4) * P:(m % 4 + 1) * P], src[:, k, :],
                                         start=(k == 0), stop=(k == KC - 1))
                    (item_used if m % 4 == 3 else pe_done).up(last)

                seen = (item_used, item_used.n) if m % 4 == 3 else (pe_done, pe_done.n)

                @block.vector
                def _(dve):
                    dve.wait_ge(seen[0].h, seen[1])
                    gated_add(dve, m, b, gate, tmp)
                freed[m] = dve_done.n

        def swa():
            with ExitStack() as c:
                qkv = sb("qkv", [P, 3, 1536], c=c)
                qT = sb("qT", [P, 8, SEQ], c=c)
                qs = sb("qs", [P, DB, 2, G, DT], c=c)
                kT = sb("kT", [P, 2, T], c=c)
                vc = sb("vc", [P, DB, 256], c=c)
                kcT = sb("kcT", [P, DB, 2, P], c=c)
                sinkr = sb("sinkr", [P, HEADS], c=c)
                sinkc = sb("sinkc", [P, 1], c=c)
                ada_sb = sb("ada_sb", [P, P], c=c)
                tmp = sb("tmp64", [P, NS], c=c)
                cK, cV = a["cache_swa_k"][0], a["cache_swa_v"][0]

                const_load("swa", c)
                with ExitStack() as c1:
                    kc = sb("kc", [P, DB, 256], c=c1)
                    r4 = [sb(f"rot{i}", [P, 20, 32], c=c1) for i in range(4)]

                    @block.gpsimd
                    def _(pool):
                        def load(dst, src):
                            aux_in.up(pool.dma_start(dst, src), 16)

                        load(kc[:, :, :], cK.rearrange("b s h d -> s b (h d)"))
                        load(vc[:, :, :], cV.rearrange("b s h d -> s b (h d)"))
                        load(sinkr[:, :], a["swa_sinks"].to_broadcast([P, HEADS]))
                        for h in range(HEADS):
                            load(sinkc[8 * h:8 * h + 8, :], a["swa_sinks"][0:1, h:h + 1].to_broadcast([DT, 1]))
                        load(router[:, :, :], a["moe_router"][0].rearrange("(k p) n -> p k n", p=P))
                        for new, old in ((a["swa_k_sample"][0], cK), (a["swa_v_sample"][0], cV)):
                            stored.up(pool.dma_start(new[:, 0:WIN - DT].rearrange("b s h d -> b s (h d)"),
                                                     old[:, DT:WIN].rearrange("b s h d -> b s (h d)")), 16)

                    for r in range(12):
                        ada_round(0, r, ada_sb)
                    ada_finish(0)
                    norm(mod[0][:, 8:16, :], mod[0][:, 0:8, :])

                    freed = {}
                    n = 0
                    for cch in range(3):
                        for t, (t0, tn) in enumerate(TILES):
                            b = bank[n % 4]
                            slot = qkv_slots[cch]

                            @block.tensor
                            def _(pe):
                                if n == 0:
                                    act_done.wait(pe)
                                    dve_done.wait(pe)
                                if n >= 4:
                                    pe.wait_ge(*freed[n - 4])
                                if t == 0:
                                    slot_in[slot].wait(pe, qkv_in[cch])
                                for k in range(KC):
                                    last = pe.matmul(b[0:tn, :], hT[:, k, t0:t0 + tn], item(slot)[:, k, :],
                                                     start=(k == 0), stop=(k == KC - 1))
                                (item_used if t == 2 else pe_done).up(last)
                            seen = (item_used.h, item_used.n) if t == 2 else (pe_done.h, pe_done.n)
                            o, i = qkv[0:tn, t, 512 * cch:512 * cch + 512], b[0:tn, :]
                            if cch < 2:
                                o = o.rearrange("p (g h d) -> p h g d", h=2, d=HD)
                                i = i.rearrange("p (h g d) -> p h g d", h=2, d=HD)
                            if n % 2 == 0:
                                @block.scalar
                                def _(act):
                                    act.wait_ge(*seen)
                                    act_done.up(act.copy(o, i))
                                freed[n] = (act_done.h, act_done.n)
                            else:
                                @block.vector
                                def _(dve):
                                    dve.wait_ge(*seen)
                                    dve_done.up(dve.tensor_copy(o, i))
                                freed[n] = (dve_done.h, dve_done.n)
                            n += 1

                    aux_kc = aux_in.n
                    for bq in range(DB):
                        @block.tensor
                        def _(pe):
                            aux_in.wait(pe, aux_kc)
                            if bq >= 2:
                                act_done.wait(pe, kc_free[bq - 2])
                            else:
                                act_done.wait(pe)
                                dve_done.wait(pe)
                            for j in range(2):
                                last = pe.transpose(bank[4 + bq % 2][:, j * P:(j + 1) * P], kc[:, bq, j * P:(j + 1) * P], ident)
                            pe_done.up(last)
                        if bq == 0:
                            kc_free = {}

                        @block.scalar
                        def _(act):
                            pe_done.wait(act)
                            act_done.up(act.copy(kcT[:, bq, :, :], bank[4 + bq % 2][:, 0:256].rearrange("p (j s) -> p j s", s=P)))
                        kc_free[bq] = act_done.n

                    for t, (t0, tn) in enumerate(TILES):
                        @block.vector
                        def _(dve):
                            act_done.wait(dve)
                            dve_done.wait(dve)
                            v = qkv[0:tn, t, 0:1280].rearrange("p (h x d) -> p h x d", x=2, d=32)
                            x1, x2 = v[:, :, 0, :], v[:, :, 1, :]
                            cos = cc("cos")[0:tn, 32 * t:32 * t + 32].unsqueeze(1).to_broadcast([tn, 20, 32])
                            sin = cc("sin")[0:tn, 32 * t:32 * t + 32].unsqueeze(1).to_broadcast([tn, 20, 32])
                            for o, x, w in ((0, x1, cos), (1, x2, sin), (2, x2, cos), (3, x1, sin)):
                                last = dve.tensor_tensor(r4[o][0:tn, :, :], x, w, ALU.mult)
                            dve_done.up(last)
                            dve_done.wait(dve)
                            dve.tensor_tensor(x1, r4[0][0:tn, :, :], r4[1][0:tn, :, :], ALU.subtract)
                            dve_done.up(dve.tensor_tensor(x2, r4[2][0:tn, :, :], r4[3][0:tn, :, :], ALU.add))

                    @block.gpsimd
                    def _(pool):
                        dve_done.wait(pool)
                        act_done.wait(pool)
                        for dst, lo in ((a["swa_k_prompt"], 1024), (a["swa_v_prompt"], 1280)):
                            stored.up(pool.dma_start(dst[0, 0].rearrange("s h d -> s (h d)"), qkv[:, 1, lo:lo + 256]), 16)
                        for dst, lo in ((a["swa_k_sample"], 1024), (a["swa_v_sample"], 1280)):
                            for bq in range(DB):
                                stored.up(pool.dma_start(dst[0, bq, WIN - DT:WIN].rearrange("s h d -> s (h d)"),
                                                         qkv[DT * bq:DT * bq + DT, 2, lo:lo + 256]), 16)

                    free = {}
                    n = 0
                    for t, (t0, tn) in enumerate(TILES):
                        for part in range(3):
                            b = bank[n % 4]

                            @block.tensor
                            def _(pe):
                                dve_done.wait(pe)
                                if n >= 4:
                                    act_done.wait(pe, free[n - 4])
                                for j in range(4 if part < 2 else 2):
                                    if part < 2:
                                        src = qkv[0:tn, t, 512 * part + P * j:512 * part + P * (j + 1)]
                                    else:
                                        src = qkv[0:tn, t, 1024 + P * j:1024 + P * (j + 1)]
                                    last = pe.transpose(b[:, j * P:j * P + tn], src, ident[0:tn, 0:tn])
                                pe_done.up(last)

                            @block.scalar
                            def _(act):
                                pe_done.wait(act)
                                if part < 2 and t == 2:
                                    act_done.up(act.copy(qs[:, :, part, :, :].rearrange("p b g t -> p g b t"),
                                                         b.rearrange("p (g x) -> p g x", x=P)[:, :, 0:NS].rearrange("p g (b t) -> p g b t", t=DT)))
                                elif part < 2:
                                    act_done.up(act.copy(qT[:, 4 * part:4 * part + 4, t0:t0 + tn],
                                                         b.rearrange("p (j t) -> p j t", t=P)[:, :, 0:tn]))
                                else:
                                    act_done.up(act.copy(kT[:, :, t0:t0 + tn],
                                                         b.rearrange("p (j t) -> p j t", t=P)[:, 0:2, 0:tn]))
                            free[n] = act_done.n
                            n += 1
                    barrier()

                sc = [sb(f"sc{i}", [P, 2, 256], c=c) for i in range(2)]
                pT = [sb(f"pT{i}", [P, 4, P], c=c) for i in range(2)]
                st = sb("st", [P, 2, 8, 2], c=c)
                units = [("prompt", nb, ch) for nb in range(2) for ch in range(8)] + [("sample", bq, 0) for bq in range(DB)]
                U = len(units)
                s_sc, s_nm, s_ex, s_pr, s_tr, s_pt, s_pv, s_ot, s_st = (flag(x) for x in (
                    "att_scores", "att_negmax", "att_exps", "att_probs", "att_transposed", "att_probsT", "att_out", "att_outT", "att_stat"))
                oT = hT

                def shape(u):
                    kind, x, ch = units[u]
                    if kind == "prompt":
                        return 2, (1 + x) * P
                    return 1, P + NS

                def scores(u):
                    kind, x, ch = units[u]
                    nh, nk = shape(u)
                    bk = pair[u % 2]

                    @block.tensor
                    def _(pe):
                        if u >= 2:
                            s_nm.wait(pe, u - 1)
                        if kind == "prompt":
                            for hf in range(2):
                                last = pe.matmul(bk[:, hf, 0:nk], qT[64 * hf:64 * hf + 64, ch, P * x:P * x + P],
                                                 kT[64 * hf:64 * hf + 64, ch // 4, 0:nk], start=True, stop=True)
                        else:
                            for kv in range(KVH):
                                cp, lo = kv // 2, 64 * (kv % 2)
                                q = qs[lo:lo + 64, x, cp, :, :].rearrange("p g t -> p (g t)")
                                pe.matmul(bk[32 * kv:32 * kv + 32, 0, 0:P], q, kcT[lo:lo + 64, x, cp, :], start=True, stop=True)
                                last = pe.matmul(bk[32 * kv:32 * kv + 32, 0, P:P + NS], q, kT[lo:lo + 64, cp, SEQ:T], start=True, stop=True)
                        s_sc.up(last)

                    @block.vector
                    def _(dve):
                        s_sc.wait(dve, u + 1)
                        if u >= 2:
                            s_tr.wait(dve, u - 1)
                        s = sc[u % 2]
                        if kind == "prompt":
                            m = cc("mask1" if x else "mask0").unsqueeze(1).to_broadcast([P, 2, nk])
                            s_st.up(dve.scalar_tensor_tensor(s[:, :, 0:nk], bk[:, :, 0:nk], HD ** -0.5, m,
                                                             ALU.mult, ALU.add))
                            sink = sink_ap(u)
                        else:
                            dve.scalar_tensor_tensor(s[:, 0, 0:P], bk[:, 0, 0:P], HD ** -0.5, cc("maskc"), ALU.mult, ALU.add)
                            s_st.up(dve.scalar_tensor_tensor(s[:, 0, P:P + NS], bk[:, 0, P:P + NS], HD ** -0.5,
                                                             cc("maskn")[:, 56 - DT * x:120 - DT * x], ALU.mult, ALU.add))
                            sink = sink_ap(u)
                        s_st.wait(dve)
                        q = st[:, u % 2, :, 0:nh]
                        s_st.up(dve.tensor_reduce(q[:, 0, :], s[:, 0:nh, 0:nk], AX.X, ALU.max))
                        s_st.wait(dve)
                        s_st.up(dve.tensor_tensor(q[:, 1, :], q[:, 0, :], sink, ALU.max))
                        s_st.wait(dve)
                        s_nm.up(dve.tensor_scalar(q[:, 1, :], q[:, 1, :], -1.0, None, ALU.mult))

                    @block.scalar
                    def _(act):
                        s_nm.wait(act, u + 1)
                        s = sc[u % 2]
                        q = st[:, u % 2, :, :]
                        for h in range(nh):
                            act.activation(s[:, h, 0:nk], s[:, h, 0:nk], ACT.Exp, bias=q[:, 1, h:h + 1], accum_out=q[:, 2, h:h + 1])
                            last = act.activation(q[:, 3, h:h + 1], sink_ap(u)[:, h:h + 1], ACT.Exp, bias=q[:, 1, h:h + 1])
                        s_ex.up(last)

                def sink_ap(u):
                    kind, x, ch = units[u]
                    if kind == "prompt":
                        h0 = 2 * (ch // 4) * G + ch % 4
                        return sinkr[:, h0:h0 + G + 1:G]
                    return sinkc[:, 0:1]

                def probs(u):
                    nh, nk = shape(u)

                    @block.vector
                    def _(dve):
                        s_ex.wait(dve, u + 1)
                        q = st[:, u % 2, :, 0:nh]
                        s_st.up(dve.tensor_tensor(q[:, 4, :], q[:, 2, :], q[:, 3, :], ALU.add))
                        s_st.wait(dve)
                        s_st.up(dve.reciprocal(q[:, 5, :], q[:, 4, :]))
                        s_st.wait(dve)
                        s = sc[u % 2][:, 0:nh, 0:nk]
                        s_pr.up(dve.tensor_tensor(s, s, q[:, 5, :].unsqueeze(2).to_broadcast([P, nh, nk]), ALU.mult))

                def transposed(u):
                    nh, nk = shape(u)
                    b = bank[4]
                    n_pieces = [(h, j) for h in range(nh) for j in range(-(-nk // P))]

                    @block.tensor
                    def _(pe):
                        s_pr.wait(pe, u + 1)
                        if u:
                            s_pt.wait(pe, u)
                        for h, j in n_pieces:
                            w = min(P, nk - P * j)
                            last = pe.transpose(b[0:w, (2 * h + j) * P:(2 * h + j + 1) * P], sc[u % 2][:, h, P * j:P * j + w], ident)
                        s_tr.up(last)

                    @block.scalar
                    def _(act):
                        s_tr.wait(act, u + 1)
                        if u >= 2:
                            s_pv.wait(act, u - 1)
                        if nh == 2:
                            j = nk // P
                            o = pT[u % 2].rearrange("p (h j) t -> p h j t", h=2)[:, :, 0:j, :]
                            i = b.rearrange("p (h j t) -> p h j t", h=2, t=P)[:, :, 0:j, :]
                            s_pt.up(act.copy(o, i))
                        else:
                            act.copy(pT[u % 2][:, 0, :], b[:, 0:P])
                            s_pt.up(act.copy(pT[u % 2][0:NS, 1, :], b[0:NS, P:2 * P]))

                def outputs(u):
                    kind, x, ch = units[u]
                    nh, nk = shape(u)
                    b = bank[5]

                    @block.tensor
                    def _(pe):
                        s_pt.wait(pe, u + 1)
                        if u:
                            s_ot.wait(pe, u)
                        if kind == "prompt":
                            for hf in range(2):
                                kv = 2 * (ch // 4) + hf
                                for j in range(nk // P):
                                    last = pe.matmul(b[64 * hf:64 * hf + 64, 0:P], qkv[:, j, 1280 + HD * kv:1280 + HD * kv + HD],
                                                     pT[u % 2][:, 2 * hf + j, :], start=(j == 0), stop=(j == nk // P - 1))
                        else:
                            for kv in range(KVH):
                                o = b[64 * (kv % 2):64 * (kv % 2) + 64, 32 * (kv // 2):32 * (kv // 2) + 32]
                                pe.matmul(o, vc[:, x, HD * kv:HD * kv + HD], pT[u % 2][:, 0, 32 * kv:32 * kv + 32], start=True, stop=False)
                                last = pe.matmul(o, qkv[0:NS, 2, 1280 + HD * kv:1280 + HD * kv + HD], pT[u % 2][0:NS, 1, 32 * kv:32 * kv + 32],
                                                 start=False, stop=True)
                        s_pv.up(last)

                    @block.vector
                    def _(dve):
                        s_pv.wait(dve, u + 1)
                        if kind == "prompt":
                            s_ot.up(dve.tensor_copy(oT[:, ch, P * x:P * x + P], b[:, 0:P]))
                        else:
                            s_ot.up(dve.tensor_copy(oT[:, :, SEQ + DT * x:SEQ + DT * x + DT],
                                                    b[:, 0:64].rearrange("p (c t) -> p c t", t=DT)))

                for i in range(U + 2):
                    if i < U:
                        scores(i)
                    if 1 <= i <= U:
                        probs(i - 1)
                        transposed(i - 1)
                    if i >= 2:
                        outputs(i - 2)
                    if i % 2 == 1 and i < 24:
                        ada_round(1, i // 2, ada_sb)
                ada_finish(1)

                @block.tensor
                def _(pe):
                    s_ot.wait(pe, U)
                    dve_done.wait(pe)
                out_projection(wo_slots, oT, mod[0][:, 16:24, :], tmp)
                barrier()

        def gla():
            with ExitStack() as c:
                qk = sb("qk", [P, 8, T], c=c)
                vt = sb("vt", [P, 3, D], c=c)
                rs = sb("rs", [P, 3, D], c=c)
                b_ = sb("b", [P, GH, T], c=c)
                g_ = sb("g", [P, GH, T], c=c)
                wa1 = sb("wa1", [P, KC, 16], c=c)
                wa2 = sb("wa2", [16, 512], c=c)
                a1T = sb("a1T", [16, T], c=c)
                tmp = sb("tmp64", [P, NS], c=c)

                const_load("gla", c)

                @block.gpsimd
                def _(pool):
                    aux_in.up(pool.dma_start(wa1[:, :, :], a["gla_wa1"][0].rearrange("(k p) n -> p k n", p=P)), 16)
                    aux_in.up(pool.dma_start(wa2[:, :], a["gla_wa2"][0]), 16)
                    aux_in.up(pool.dma_start(router[:, :, :], a["moe_router"][1].rearrange("(k p) n -> p k n", p=P)), 16)

                norm(mod[1][:, 8:16, :], mod[1][:, 0:8, :])

                @block.tensor
                def _(pe):
                    act_done.wait(pe)
                    dve_done.wait(pe)
                    aux_in.wait(pe)

                @block.tensor
                def _(pe):
                    for k in range(KC):
                        last = pe.matmul(bank[7][0:16, 0:T], wa1[:, k, :], hT[:, k, :], start=(k == 0), stop=(k == KC - 1))
                    pe_done.up(last)

                @block.scalar
                def _(act):
                    pe_done.wait(act)
                    act_done.up(act.copy(a1T[:, :], bank[7][0:16, 0:T]))

                for h in range(GH):
                    @block.tensor
                    def _(pe):
                        act_done.wait(pe)
                        pe_done.up(pe.matmul(bank[6 + h % 2][:, 0:T], wa2[:, h * P:(h + 1) * P], a1T[:, :], start=True, stop=True))

                    @block.scalar
                    def _(act):
                        pe_done.wait(act)
                        act_done.up(act.activation(g_[:, h, :], bank[6 + h % 2][:, 0:T], ACT.Identity, bias=vt2[:, V2_BA + h:V2_BA + h + 1]))

                @block.vector
                def _(dve):
                    act_done.wait(dve)
                    dve_done.up(dve.tensor_scalar(b_[:, :, :], g_[:, :, :], -1.0, None, ALU.mult))
                    dve_done.wait(dve)
                    dve_done.up(dve.tensor_tensor(b_[:, :, :], b_[:, :, :], g_[:, :, :], ALU.min))

                @block.scalar
                def _(act):
                    dve_done.wait(act)
                    act_done.up(act.activation(b_[:, :, :], b_[:, :, :], ACT.Exp))
                    act_done.wait(act)
                    act_done.up(act.activation(b_[:, :, :], b_[:, :, :], ACT.Ln, bias=1.0))

                @block.vector
                def _(dve):
                    act_done.wait(dve)
                    dve_done.up(dve.scalar_tensor_tensor(g_[:, :, :], g_[:, :, :], 0.0, b_[:, :, :], ALU.min, ALU.subtract))
                    dve_done.wait(dve)
                    dve_done.up(dve.tensor_scalar(g_[:, :, :], g_[:, :, :], 1.0 / 16.0, None, ALU.mult))
                    dve_done.wait(dve)
                    for h in range(GH):
                        dve_done.up(dve.tensor_tensor_scan(b_[:, h, :], cc("reset"), g_[:, h, :], 0.0, ALU.mult, ALU.add))

                freed = {}
                n = 0
                for cch in range(6):
                    slot = win_slots[cch]
                    for j in range(4 if cch < 2 else 3):
                        b = bank[n % 4]
                        ends = j == (3 if cch < 2 else 2)

                        @block.tensor
                        def _(pe):
                            if n >= 4:
                                pe.wait_ge(*freed[n - 4])
                            if j == 0:
                                slot_in[slot].wait(pe, win_in[cch])
                            for k in range(KC):
                                w = item(slot)[:, k, :]
                                if cch < 2:
                                    last = pe.matmul(b[:, 0:T], w[:, j * P:(j + 1) * P], hT[:, k, :], start=(k == 0), stop=(k == KC - 1))
                                else:
                                    t0, tn = TILES[j]
                                    last = pe.matmul(b[0:tn, :], hT[:, k, t0:t0 + tn], w, start=(k == 0), stop=(k == KC - 1))
                            (item_used if ends else pe_done).up(last)
                        seen = (item_used.h, item_used.n) if ends else (pe_done.h, pe_done.n)
                        if cch < 2:
                            @block.scalar
                            def _(act):
                                act.wait_ge(*seen)
                                act_done.up(act.activation(qk[:, 4 * cch + j, :], b[:, 0:T], ACT.Copy, scale=DK ** -0.5 if cch == 0 else 1.0))
                            freed[n] = (act_done.h, act_done.n)
                        elif cch < 4:
                            tn = TILES[j][1]

                            @block.vector
                            def _(dve):
                                dve.wait_ge(*seen)
                                dve_done.up(dve.tensor_copy(vt[0:tn, j, 512 * (cch - 2):512 * (cch - 1)], b[0:tn, :]))
                            freed[n] = (dve_done.h, dve_done.n)
                        else:
                            tn = TILES[j][1]

                            @block.scalar
                            def _(act):
                                act.wait_ge(*seen)
                                act_done.up(act.activation(rs[0:tn, j, 512 * (cch - 4):512 * (cch - 3)], b[0:tn, :], ACT.Silu))
                            freed[n] = (act_done.h, act_done.n)
                        n += 1

                eb = g_
                nb = sb("nb", [P, GH, T], c=c)

                @block.scalar
                def _(act):
                    dve_done.wait(act)
                    act_done.up(act.activation(eb[:, :, :], b_[:, :, :], ACT.Exp))

                @block.vector
                def _(dve):
                    dve_done.wait(dve)
                    dve_done.up(dve.tensor_scalar(nb[:, :, :], b_[:, :, :], -1.0, None, ALU.mult))

                s0 = sb("s0", [P, DB, DV], c=c)
                sp_ = sb("sp", [P, DV], c=c)
                ke = sb("ke", [P, 8, P], c=c)
                qz = sb("qz", [P, DB, NS], c=c)
                qe = sb("qe", [P, P], c=c)
                qi = sb("qi", [P, T], c=c)
                kd = sb("kd", [P, P], c=c)
                kdt = sb("kdt", [P, P], c=c)
                km = ke
                km2 = sb("km2", [NS, DB, P], c=c)
                at = sb("at", [P, P], c=c)
                stt = sb("stt", [P, 4], c=c)
                junk = sb("junk", [P, DV], c=c)

                @block.vector
                def _(dve):
                    dve.memset(ke[:, :, :], 0.0)
                    dve_done.up(dve.memset(qz[:, :, :], 0.0))

                def head_norm(h, t):
                    tn = TILES[t][1]
                    r_ = rs[0:tn, t, DV * h:DV * (h + 1)]

                    @block.scalar
                    def _(act):
                        pe_done.wait(act)
                        dve_done.wait(act)
                        act_done.up(act.activation(junk[0:tn, :], bank[2][0:tn, 0:DV], ACT.Square, accum_out=stt[0:tn, 0:1]))

                    @block.vector
                    def _(dve):
                        act_done.wait(dve)
                        dve_done.up(dve.tensor_scalar(stt[0:tn, 1:2], stt[0:tn, 0:1], 1.0 / DV, EPS, ALU.mult, ALU.add))
                        dve_done.wait(dve)
                        dve_done.up(dve.reciprocal(stt[0:tn, 2:3], stt[0:tn, 1:2]))

                    @block.scalar
                    def _(act):
                        dve_done.wait(act)
                        act_done.up(act.activation(stt[0:tn, 3:4], stt[0:tn, 2:3], ACT.Sqrt))

                    @block.vector
                    def _(dve):
                        act_done.wait(dve)
                        dve_done.up(dve.scalar_tensor_tensor(r_, bank[2][0:tn, 0:DV], stt[0:tn, 3:4], r_, ALU.mult, ALU.mult))

                for h in range(GH):
                    q_, k_, v_ = qk[:, h, :], qk[:, 4 + h, :], vt[:, :, DV * h:DV * (h + 1)]

                    @block.gpsimd
                    def _(pool):
                        dve_done.wait(pool)
                        stored.wait(pool)
                        aux_in.up(pool.dma_start(s0[:, :, :], a["state_gla"][0, :, h].rearrange("b d e -> d b e")), 16)

                    @block.vector
                    def _(dve):
                        act_done.wait(dve)
                        dve_done.wait(dve)
                        pe_done.wait(dve)
                        dve_done.up(dve.tensor_tensor(qi[:, :], q_, eb[:, h, :], ALU.mult))

                    for n in range(2):
                        c0_ = P * n

                        @block.scalar
                        def _(act):
                            dve_done.wait(act)
                            pe_done.wait(act)
                            for i in range(8):
                                ref = c0_ + 16 * i - 1
                                rp = b_[:, h, ref:ref + 1] if i else 0.0
                                rn = nb[:, h, ref:ref + 1] if i else 0.0
                                act.activation(ke[:, i, 0:16 * (i + 1)], b_[:, h, c0_:c0_ + 16 * (i + 1)], ACT.Exp, bias=rp, scale=-1.0)
                                act.activation(qe[:, 16 * i:16 * i + 16], b_[:, h, c0_ + 16 * i:c0_ + 16 * i + 16], ACT.Exp, bias=rn)
                            act_done.up(act.activation(kd[:, :], b_[:, h, c0_:c0_ + P], ACT.Exp, bias=b_[:, h, c0_ + P - 1:c0_ + P], scale=-1.0))

                        @block.vector
                        def _(dve):
                            act_done.wait(dve)
                            dve.tensor_tensor(ke[:, :, :], ke[:, :, :], k_[:, c0_:c0_ + P].unsqueeze(1).to_broadcast([P, 8, P]), ALU.mult)
                            dve.tensor_tensor(qe[:, :], qe[:, :], q_[:, c0_:c0_ + P], ALU.mult)
                            dve_done.up(dve.tensor_tensor(kd[:, :], kd[:, :], k_[:, c0_:c0_ + P], ALU.mult))

                        @block.tensor
                        def _(pe):
                            dve_done.wait(pe)
                            for i in range(8):
                                pe.matmul(bank[0][:, 16 * i:16 * i + 16], ke[:, i, :], qe[:, 16 * i:16 * i + 16], start=True, stop=True)
                            pe_done.up(pe.transpose(bank[1][:, 0:P], kd[:, :], ident))

                        @block.vector
                        def _(dve):
                            pe_done.wait(dve)
                            dve_done.up(dve.tensor_tensor(at[:, :], bank[0][:, 0:P], cc("tri"), ALU.mult))

                        @block.scalar
                        def _(act):
                            pe_done.wait(act)
                            act_done.up(act.copy(kdt[:, :], bank[1][:, 0:P]))

                        @block.tensor
                        def _(pe):
                            dve_done.wait(pe)
                            act_done.wait(pe)
                            pe.matmul(bank[2][:, 0:DV], at[:, :], v_[:, n, :], start=True, stop=(n == 0))
                            if n:
                                pe.matmul(bank[2][:, 0:DV], qi[:, c0_:c0_ + P], sp_[:, :], start=False, stop=True)
                            pe_done.up(pe.matmul(bank[3][:, 0:DV], kdt[:, :], v_[:, n, :], start=True, stop=True))

                        @block.vector
                        def _(dve):
                            pe_done.wait(dve)
                            if n == 0:
                                if h:
                                    stored.wait(dve)
                                dve_done.up(dve.tensor_copy(sp_[:, :], bank[3][:, 0:DV]))
                            else:
                                dve_done.up(dve.scalar_tensor_tensor(sp_[:, :], sp_[:, :], eb[:, h, c0_ + P - 1:c0_ + P], bank[3][:, 0:DV],
                                                                     ALU.mult, ALU.add))
                        head_norm(h, n)

                    @block.gpsimd
                    def _(pool):
                        dve_done.wait(pool)
                        stored.up(pool.dma_start(a["gla_state_prompt"][0, 0, h], sp_[:, :]), 16)

                    bs = b_[:, h, SEQ:T].rearrange("p (b t) -> p b t", t=DT)

                    @block.vector
                    def _(dve):
                        pe_done.wait(dve)
                        dve_done.wait(dve)
                        dve.tensor_tensor(kd[:, 0:NS].rearrange("p (b t) -> p b t", t=DT),
                                          bs[:, :, DT - 1:DT].to_broadcast([P, DB, DT]), bs, ALU.subtract)
                        for bq in range(DB):
                            last = dve.tensor_copy(qz[:, bq, DT * bq:DT * bq + DT], qi[:, SEQ + DT * bq:SEQ + DT * bq + DT])
                        dve_done.up(last)

                    @block.scalar
                    def _(act):
                        dve_done.wait(act)
                        act.activation(kd[:, 0:NS], kd[:, 0:NS], ACT.Exp)
                        act_done.up(act.activation(qe[:, 0:NS], b_[:, h, SEQ:T], ACT.Exp, scale=-1.0))

                    @block.vector
                    def _(dve):
                        act_done.wait(dve)
                        dve.tensor_tensor(kd[:, 0:NS], kd[:, 0:NS], k_[:, SEQ:T], ALU.mult)
                        dve_done.up(dve.tensor_tensor(qe[:, 0:NS], qe[:, 0:NS], k_[:, SEQ:T], ALU.mult))

                    @block.tensor
                    def _(pe):
                        dve_done.wait(pe)
                        pe.matmul(bank[0][0:NS, 0:NS], qe[:, 0:NS], qi[:, SEQ:T], start=True, stop=True)
                        pe_done.up(pe.transpose(bank[1][0:NS, 0:P], kd[:, 0:NS], ident))

                    @block.vector
                    def _(dve):
                        pe_done.wait(dve)
                        dve.tensor_tensor(at[0:NS, 0:NS], bank[0][0:NS, 0:NS], cc("tri8")[0:NS, :], ALU.mult)
                        dve_done.up(dve.tensor_tensor(km2[:, :, :], bank[1][0:NS, 0:P].unsqueeze(1).to_broadcast([NS, DB, P]),
                                                      cc("rowsel")[0:NS, :].unsqueeze(2).to_broadcast([NS, DB, P]), ALU.mult))

                    @block.tensor
                    def _(pe):
                        dve_done.wait(pe)
                        aux_in.wait(pe)
                        pe.matmul(bank[2][0:NS, 0:DV], at[0:NS, 0:NS], v_[0:NS, 2, :], start=True, stop=False)
                        for bq in range(DB):
                            last = pe.matmul(bank[2][0:NS, 0:DV], qz[:, bq, :], s0[:, bq, :], start=False, stop=(bq == DB - 1))
                        pe_done.up(last)
                    head_norm(h, 2)
                    def bk(bq):
                        return bank[4 + bq // 2][:, DV * (bq % 2):DV * (bq % 2) + DV]

                    @block.tensor
                    def _(pe):
                        dve_done.wait(pe)
                        for bq in range(DB):
                            last = pe.matmul(bk(bq), km2[:, bq, :], v_[0:NS, 2, :], start=True, stop=True)
                        pe_done.up(last)

                    @block.vector
                    def _(dve):
                        pe_done.wait(dve)
                        for bq in range(DB):
                            e = SEQ + DT * bq + DT - 1
                            last = dve.scalar_tensor_tensor(s0[:, bq, :], s0[:, bq, :], eb[:, h, e:e + 1], bk(bq), ALU.mult, ALU.add)
                        dve_done.up(last)

                    @block.gpsimd
                    def _(pool):
                        dve_done.wait(pool)
                        stored.up(pool.dma_start(a["gla_state_sample"][0, :, h].rearrange("b d e -> d b e"), s0[:, :, :]), 16)

                free = {}
                for k in range(KC):
                    b = bank[k % 2]

                    @block.tensor
                    def _(pe):
                        dve_done.wait(pe)
                        if k >= 2:
                            act_done.wait(pe, free[k - 2])
                        for t, (t0, tn) in enumerate(TILES):
                            last = pe.transpose(b[:, t0:t0 + tn], rs[0:tn, t, k * P:(k + 1) * P], ident[0:tn, 0:tn])
                        pe_done.up(last)

                    @block.scalar
                    def _(act):
                        pe_done.wait(act)
                        act_done.up(act.activation(hT[:, k, :], b[:, 0:T], ACT.Copy, scale=vt2[:, V2_GN + k % 2:V2_GN + k % 2 + 1]))
                    free[k] = act_done.n

                @block.tensor
                def _(pe):
                    act_done.wait(pe)
                out_projection(gwo_slots, hT, mod[1][:, 16:24, :], tmp)
                barrier()

        moe_sems = {}
        BASE = 1
        LOOP_SEMS = ("sel_ready", "gather_full", "gather_act", "gather_dve", "onehotT_psum", "onehotT_ready",
                     "slotw_psum", "slotw_ready", "gu_ready", "silu_ready", "h_ready", "hT_psum", "hT_ready",
                     "y_psum", "y_high", "y_low", "sum_psum", "sum_added")

        def msem(name):
            if name not in moe_sems:
                moe_sems[name] = sem(name)
            return moe_sems[name]

        def moe(l):
            at_layer[0] = l
            wg, wu, wd = a["moe_wg"][l], a["moe_wu"][l], a["moe_wd"][l]
            with ExitStack() as c:
                htok = sb("htok", [P, 2, 2, D], F32R, c=c)
                htok2 = sb("htok2", [P, D], F32R, c=c)
                posm = sb("posm", [P, 3, NE + 8], c=c)
                wgt = sb("wgt", [P, 3, NE + 8], c=c)
                wpart = sb("wpart", [P, 5, NE + 8], F32R, c=c)
                wov = sb("wov", [P, 3, NE], c=c)
                cnt = sb("cnt", [P, NE], I32, c=c)
                with ExitStack() as c1:
                    sco, slc, mk, ws = (sb(n, [P, 3, NE], c=c1) for n in ("sco", "slc", "mk", "ws"))
                    mb = sb("mb", [P, 3, NE], BF16, c=c1)
                    t8 = sb("t8", [P, 3, 8, 8], c=c1)
                    gs = sb("gs", [P, 3, 8], c=c1)
                    gc = sb("gcmp", [P, 3, 8], c=c1)
                    rk = sb("rk", [P, 8, 8], c=c1)
                    rk2 = sb("rk2", [P, 8, 8], c=c1)
                    m8 = sb("m8", [P, 3, 8], c=c1)
                    sm = sb("sm", [P, 3, 2], c=c1)

                    norm(mod[l][:, 32:40, :], mod[l][:, 24:32, :])

                    @block.tensor
                    def _(pe):
                        act_done.wait(pe)
                        dve_done.wait(pe)
                        aux_in.wait(pe)
                        for t, (t0, tn) in enumerate(TILES):
                            for k in range(KC):
                                last = pe.matmul(bank[6][0:tn, NE * t:NE * t + NE], hT[:, k, t0:t0 + tn], router[:, k, :],
                                                 start=(k == 0), stop=(k == KC - 1))
                        pe_done.up(last)

                    @block.scalar
                    def _(act):
                        pe_done.wait(act)
                        act.activation(sco[:, 0:2, :], bank[6][:, 0:2 * NE].rearrange("p (t e) -> p t e", e=NE), ACT.Sigmoid)
                        act_done.up(act.activation(sco[0:NS, 2, :], bank[6][0:NS, 2 * NE:3 * NE], ACT.Sigmoid))

                    free = {}
                    for n, (t, k4) in enumerate((t, k4) for t in range(3) for k4 in range(2)):
                        b = bank[n % 4]
                        t0, tn = TILES[t]

                        @block.tensor
                        def _(pe):
                            if n >= 4:
                                dve_done.wait(pe, free[n - 4])
                            for j in range(4):
                                last = pe.transpose(b[0:tn, j * P:(j + 1) * P], hT[:, 4 * k4 + j, t0:t0 + tn], ident)
                            pe_done.up(last)
                        hi = htok[:, t, 0, :] if t < 2 else htok2[0:NS, :]
                        lo = htok[:, t, 1, :] if t < 2 else htok2[NS:P, :]
                        hi, lo = hi[:, 512 * k4:512 * k4 + 512], lo[:, 512 * k4:512 * k4 + 512]

                        @block.scalar
                        def _(act):
                            pe_done.wait(act)
                            act_done.up(act.copy(hi, b[0:tn, :]))

                        @block.vector
                        def _(dve):
                            act_done.wait(dve)
                            dve_done.up(dve.tensor_tensor(lo, b[0:tn, :], hi.bitcast(F32), ALU.subtract))
                        free[n] = dve_done.n

                    @block.vector
                    def _(dve):
                        def then(ins):
                            dve_done.up(ins)
                            dve_done.wait(dve)

                        act_done.wait(dve)
                        for t, (t0, tn) in enumerate(TILES):
                            s_, l_, m_, w_ = sco[0:tn, t, :], slc[0:tn, t, :], mk[0:tn, t, :], ws[0:tn, t, :]
                            g3 = l_.rearrange("p (g e) -> p g e", e=8)
                            then(dve.tensor_tensor(l_, s_, biasr[0:tn, l, :], ALU.add))
                            for g in range(NGRP):
                                last = dve.max(t8[0:tn, t, g, :], l_[:, 8 * g:8 * g + 8])
                            then(last)
                            then(dve.tensor_tensor(gs[0:tn, t, :], t8[0:tn, t, :, 0], t8[0:tn, t, :, 1], ALU.add))
                            me = gs[0:tn, t, :].unsqueeze(2).to_broadcast([tn, 8, 8])
                            other = gs[0:tn, t, :].unsqueeze(1).to_broadcast([tn, 8, 8])
                            dve.tensor_tensor(rk[0:tn, :, :], other, me, ALU.is_gt)
                            then(dve.tensor_tensor(rk2[0:tn, :, :], other, me, ALU.is_equal))
                            then(dve.tensor_tensor(rk2[0:tn, :, :], rk2[0:tn, :, :], cc("tie")[0:tn, :].rearrange("p (a b) -> p a b", b=8), ALU.mult))
                            then(dve.tensor_tensor(rk[0:tn, :, :], rk[0:tn, :, :], rk2[0:tn, :, :], ALU.add))
                            then(dve.tensor_reduce(gc[0:tn, t, :], rk[0:tn, :, :], AX.X, ALU.add))
                            then(dve.tensor_scalar(gc[0:tn, t, :], gc[0:tn, t, :], 4.0, None, ALU.is_lt))
                            gm = gc[0:tn, t, :].unsqueeze(2).to_broadcast([tn, 8, 8])
                            then(dve.tensor_tensor(g3, g3, gm, ALU.mult))
                            then(dve.tensor_scalar(gc[0:tn, t, :], gc[0:tn, t, :], 1.0, -NEG, ALU.subtract, ALU.mult))
                            then(dve.tensor_tensor(g3, g3, gm, ALU.add))
                            then(dve.max(m8[0:tn, t, :], l_))
                            then(dve.match_replace(m_, m8[0:tn, t, :], l_, 3 * NEG))
                            then(dve.tensor_tensor(m_, m_, l_, ALU.not_equal))
                            dve.tensor_copy(mb[0:tn, t, :], m_)
                            then(dve.tensor_tensor(w_, s_, m_, ALU.mult))
                            then(dve.tensor_reduce(sm[0:tn, t, 0:1], w_, AX.X, ALU.add))
                            then(dve.reciprocal(sm[0:tn, t, 1:2], sm[0:tn, t, 0:1]))
                            then(dve.tensor_scalar(w_, w_, sm[0:tn, t, 1:2], 2.5, ALU.mult, ALU.mult))

                    @block.tensor
                    def _(pe):
                        dve_done.wait(pe)
                        b = bank[7]
                        up, up2, on = upper_b[:, 0, :], upper_b[:, 1, :], upper_b[:, 2, :]
                        pe.matmul(b[:, 0:64], up, mb[:, 0, :], start=True, stop=True)
                        pe.matmul(b[:, 64:128], on, mb[:, 0, :], start=True, stop=False)
                        pe.matmul(b[:, 64:128], up, mb[:, 1, :], start=False, stop=True)
                        for lo in (128, 192):
                            pe.matmul(b[:, lo:lo + 64], on, mb[:, 0, :], start=True, stop=False)
                            pe.matmul(b[:, lo:lo + 64], on, mb[:, 1, :], start=False, stop=False)
                            last = pe.matmul(b[:, lo:lo + 64], (up2 if lo == 128 else on)[0:NS, :], mb[0:NS, 2, :], start=False, stop=True)
                        pe_done.up(last)

                    @block.vector
                    def _(dve):
                        def then(ins):
                            dve_done.up(ins)
                            dve_done.wait(dve)

                        dve.memset(posm[:, :, NE:], BIG)
                        dve.memset(wgt[:, :, :], 0.0)
                        dve.tensor_copy(mk[NS:P, 2, :], mk[0:NS, 2, :])
                        then(dve.tensor_copy(ws[NS:P, 2, :], ws[0:NS, 2, :]))
                        pe_done.wait(dve)
                        p_ = posm[:, :, 0:NE]
                        then(dve.scalar_tensor_tensor(p_, bank[7][:, 0:192].rearrange("p (t e) -> p t e", e=NE), -BIG, mk[:, :, :],
                                                      ALU.add, ALU.mult))
                        then(dve.tensor_scalar(p_, p_, BIG, None, ALU.add))
                        dve.tensor_copy(cnt[:, :], bank[7][:, 192:256])
                        dve.tensor_copy(wgt[:, :, 0:NE], ws[:, :, :])
                        then(dve.tensor_scalar(wov[:, :, :], p_, float(CAP), None, ALU.is_ge))
                        then(dve.tensor_tensor(wov[:, :, :], wov[:, :, :], ws[:, :, :], ALU.mult))
                        for t in range(2):
                            then(dve.tensor_copy(wpart[:, 2 * t, :], wgt[:, t, :]))
                            then(dve.tensor_tensor(wpart[:, 2 * t + 1, :], wgt[:, t, :], wpart[:, 2 * t, :].bitcast(F32), ALU.subtract))
                        then(dve.tensor_copy(wpart[:, 4, :], wgt[:, 2, :]))
                        then(dve.tensor_tensor(wpart[NS:P, 4, :], wgt[NS:P, 2, :], wpart[NS:P, 4, :].bitcast(F32), ALU.subtract))
                    barrier()

                sel = [sb(f"sel{i}", [P, 3, 4 * CAP], F32R, c=c) for i in range(2)]
                gt = [sb(f"gt{i}", [P, 2, T], F32R, c=c) for i in range(2)]
                yst = sb("yst", [P, 2, D], F32R, c=c)
                xg = [sb(f"xg{i}", [P, KC, 4 * CAP], c=c) for i in range(2)]
                acc = sb("acc", [P, KC, T], c=c)
                sg = sb("sg", [P, FF], c=c)
                hh = sb("hh", [P, FF], c=c)
                hTs = [sb(f"hTs{i}", [P, 2, P], c=c) for i in range(2)]
                wsl = [sb(f"wsl{i}", [P, 2], c=c) for i in range(2)]
                dg = sb("dg", [P, P], c=c)
                ovh = sb("ovh", [P, 2, T], c=c)
                wrow = sb("wrow", [P, T], c=c)

                dense_pe, dense_act, dense_dve = (msem(n) for n in ("dense_products", "dense_silu", "dense_sums"))
                KPE, KACT, KDVE = 11, 2, 11

                def dense(slot, n_of, weights, first):
                    gw = ring[:, slot, 0:GUW].rearrange("p (k n) -> p k n", n=512)
                    dw = ring[:, slot, GUW:SLOT].rearrange("p (f n) -> p f n", n=D)

                    def on_pe(pe):
                        if weights is not None:
                            for t, (t0, tn) in enumerate(TILES):
                                pe.wait_ge(dense_dve, n_of(pe, KDVE + 3, t + 1))
                                last = pe.matmul(bank[3][:, t0:t0 + tn], ones[0:tn, :], dg[0:tn, 0:tn], start=True, stop=True)
                                if t < 2:
                                    last.then_inc(dense_pe, 1)
                            last.then_inc(dense_pe, 1)
                        for f in range(2):
                            if f:
                                pe.wait_ge(dense_dve, n_of(pe, KDVE + 3, 4 + 1))
                            for u, b in ((0, bank[4]), (1, bank[5])):
                                for k in range(KC):
                                    last = pe.matmul(b[:, 0:T], gw[:, k, FF * u + P * f:FF * u + P * f + P], hT[:, k, :],
                                                     start=(k == 0), stop=(k == KC - 1))
                            last.then_inc(dense_pe, 1)
                        for m in range(KC):
                            pe.wait_ge(dense_dve, n_of(pe, KDVE + 3, 6 if m < 2 else 5 + m))
                            for f in range(2):
                                last = pe.matmul(bank[4 + m % 2][:, 0:T], dw[:, f, m * P:(m + 1) * P], ovh[:, f, :], start=(f == 0), stop=(f == 1))
                            last.then_inc(dense_pe, 1)
                        pe.wait_ge(dense_dve, n_of(pe, KDVE + 3, KDVE + 3))

                    def on_act(act):
                        for f in range(2):
                            act.wait_ge(dense_pe, n_of(act, KPE + 2, 4 + f))
                            act.activation(ovh[:, f, :], bank[4][:, 0:T], ACT.Silu).then_inc(dense_act, 1)

                    def on_dve(dve):
                        if weights is not None:
                            for t, (t0, tn) in enumerate(TILES):
                                if t:
                                    dve.wait_ge(dense_pe, n_of(dve, KPE + 2, t))
                                dve.tensor_scalar(dg[0:tn, 0:tn], ident[0:tn, 0:tn], weights(dve, t)[0:tn], None, ALU.mult).then_inc(dense_dve, 1)
                            dve.wait_ge(dense_pe, n_of(dve, KPE + 2, 3))
                            dve.tensor_copy(wrow[:, :], bank[3][:, 0:T]).then_inc(dense_dve, 1)
                            dve.wait_ge(dense_dve, n_of(dve, KDVE + 3, 4))
                        for f in range(2):
                            dve.wait_ge(dense_act, n_of(dve, KACT, 1 + f))
                            if weights is not None:
                                dve.tensor_tensor(ovh[:, f, :], ovh[:, f, :], bank[5][:, 0:T], ALU.mult).then_inc(dense_mid, 1)
                                dve.wait_ge(dense_mid, n_of(dve, 2, 1 + f))
                                dve.tensor_tensor(ovh[:, f, :], ovh[:, f, :], wrow[:, :], ALU.mult).then_inc(dense_dve, 1)
                            else:
                                dve.tensor_tensor(ovh[:, f, :], ovh[:, f, :], bank[5][:, 0:T], ALU.mult).then_inc(dense_dve, 1)
                        for m in range(KC):
                            dve.wait_ge(dense_pe, n_of(dve, KPE + 2, 6 + m))
                            b = bank[4 + m % 2][:, 0:T]
                            if first:
                                dve.tensor_copy(acc[:, m, :], b).then_inc(dense_dve, 1)
                            else:
                                dve.tensor_tensor(acc[:, m, :], acc[:, m, :], b, ALU.add).then_inc(dense_dve, 1)
                        dve.wait_ge(dense_dve, n_of(dve, KDVE + 3, KDVE + 3))
                    return on_pe, on_act, on_dve

                dense_mid = msem("dense_gated")
                def run_value(eng, k, c_):
                    return eng.snap(dense_regs(eng)) * k + c_

                def shared_part(eng, part, fill):
                    r = dense_regs(eng)
                    for s_, n_ in fill:
                        eng.sem_inc(s_, n_)
                    part(eng)
                    eng.reg_add(r, r, 1)

                sh = shared_slots[l]
                on_pe, on_act, on_dve = dense(sh, run_value, None, True)

                @block.tensor
                def _(pe):
                    slot_in[sh].wait(pe, shared_in[l])
                    down_in[sh].wait(pe, shared_down[l])
                    shared_part(pe, on_pe, [(dense_pe, 3)])
                    item_used.up(pe.drain())

                @block.scalar
                def _(act):
                    shared_part(act, on_act, [])

                @block.vector
                def _(dve):
                    shared_part(dve, on_dve, [(dense_dve, 4), (dense_mid, 2)])

                S = {n: msem(n) for n in LOOP_SEMS}
                GPI = 2
                NG = NE // 4
                PASSES = NG // GPI

                class At:

                    def __init__(self, it):
                        self.it = it

                    def __call__(self, per, g, c_, extra=0):
                        return self.it * (per * GPI) + (l * (NG + extra) * per + g * per + c_ + BASE)

                def gather_pe(pe, at_, g, ms):
                    par = g % 2
                    for m2 in ms:
                        bk = bank[m2 % 2]
                        if m2 == 0:
                            pe.wait_ge(S["sel_ready"], at_(1, g, 1, 2))
                        if m2 >= 2:
                            pe.wait_ge(S["gather_act" if m2 % 2 == 0 else "gather_dve"], at_(2, g, m2 // 2, 1))
                        for m in (2 * m2, 2 * m2 + 1):
                            o = bk[:, (m % 2) * 256:(m % 2) * 256 + 256]
                            for n_, (w, s_) in enumerate(((htok[:, 0, 0, :], 0), (htok[:, 0, 1, :], 0), (htok[:, 1, 0, :], 1),
                                                          (htok[:, 1, 1, :], 1), (htok2[:, :], 2))):
                                last = pe.matmul(o, w[:, m * P:(m + 1) * P], sel[par][:, s_, :], start=(n_ == 0), stop=(n_ == 4))
                        last.then_inc(S["gather_full"], 1)

                def onehot_pe(pe, at_, g, e0):
                    par = g % 2
                    for q in range(2):
                        if q:
                            pe.wait_ge(S["onehotT_ready"], at_(2, g, 1, 1))
                        for t, (t0, tn) in enumerate(TILES):
                            last = pe.transpose(bank[6][:, t0:t0 + tn], sel[par][0:tn, t, P * q:P * q + P].bitcast(F32), ident[0:tn, 0:tn])
                        last.then_inc(S["onehotT_psum"], 1)
                    for q in range(2):
                        for n_, s_ in enumerate((0, 0, 1, 1, 2)):
                            last = pe.matmul(bank[7][:, 2 * q:2 * q + 2], sel[par][:, s_, P * q:P * q + P], wpart[:, n_, bass.ds(e0 + 2 * q, 2)],
                                             start=(n_ == 0), stop=(n_ == 4))
                    last.then_inc(S["slotw_psum"], 1)

                def gather_act(act, at_, g, m2):
                    act.wait_ge(S["gather_full"], at_(4, g, m2 + 1, 1))
                    act.copy(xg[g % 2][:, 2 * m2:2 * m2 + 2, :], bank[m2 % 2].rearrange("p (m s) -> p m s", s=256)).then_inc(S["gather_act"], 1)

                def gather_dve(dve, at_, g, m2):
                    dve.wait_ge(S["gather_full"], at_(4, g, m2 + 1, 1))
                    dve.tensor_copy(xg[g % 2][:, 2 * m2:2 * m2 + 2, :], bank[m2 % 2].rearrange("p (m s) -> p m s", s=256)).then_inc(S["gather_dve"], 1)

                def onehot_act(act, at_, g):
                    for q in range(2):
                        act.wait_ge(S["onehotT_psum"], at_(2, g, q + 1, 1))
                        act.copy(gt[g % 2][:, q, :], bank[6][:, 0:T]).then_inc(S["onehotT_ready"], 1)

                def slotw_dve(dve, at_, g):
                    dve.wait_ge(S["slotw_psum"], at_(1, g, 1, 1))
                    w = bank[7][:, 0:4].rearrange("p (q j) -> p q j", j=2)
                    dve.tensor_copy(wsl[g % 2][0:64, :], w[0:64, :, 0])
                    dve.tensor_copy(wsl[g % 2][64:P, :], w[64:P, :, 1]).then_inc(S["slotw_ready"], 1)

                def sel_dve(dve, at_, g, e0):
                    for t in range(3):
                        last = dve.tensor_tensor(sel[g % 2][:, t, :].rearrange("p (e s) -> p e s", s=CAP),
                                                 cc("slot").unsqueeze(1).to_broadcast([P, 4, CAP]),
                                                 posm[:, t, bass.ds(e0, 4)].unsqueeze(2).to_broadcast([P, 4, CAP]), ALU.is_equal)
                    last.then_inc(S["sel_ready"], 1)

                def overflow(eng, it, g, q, part_of):
                    for j in range(2):
                        s_ = 2 * q + j
                        e = it * (4 * GPI) + (4 * g + s_)
                        n_ = eng.value_load(cnt[0:1, bass.ds(e, 1)], min_val=0, max_val=T)
                        with eng.If(n_ > CAP):
                            if eng is nc.tensor:
                                eng.wait_ge(down_in[s_].h, down_expected(At(it), s_, g))
                            part = part_of(s_, e)
                            part(eng)
                            r = dense_regs(eng)
                            eng.reg_add(r, r, 1)

                def dense_of(which):
                    def part_of(s_, e):
                        parts = dense(s_, run_value, lambda dve, t: wov[:, t, bass.ds(e, 1)], False)
                        return parts[which]
                    return part_of

                zero_at = At(0)

                @block.tensor
                def _(pe):
                    gather_pe(pe, zero_at, 0, range(4))
                    onehot_pe(pe, zero_at, 0, 0)
                    with pe.Fori(0, PASSES) as it:
                        at_ = At(it)
                        for g in range(GPI):
                            e1 = it * (4 * GPI) + 4 * (g + 1)

                            def gate_up(q):
                                pe.wait_ge(S["gather_act"], at_(2, g, 2, 1))
                                pe.wait_ge(S["gather_dve"], at_(2, g, 2, 1))
                                pe.wait_ge(S["h_ready"], at_(2, g, q))
                                for j in range(2):
                                    pe.wait_ge(slot_in[2 * q + j].h, gu_expected(at_, 2 * q + j, g))
                                for k in range(KC):
                                    for j in range(2):
                                        s_ = 2 * q + j
                                        last = pe.matmul(bank[2][64 * j:64 * j + 64, :], xg[g % 2][:, k, CAP * s_:CAP * s_ + CAP],
                                                         ring[:, s_, 512 * k:512 * k + 512], start=(k == 0), stop=(k == KC - 1))
                                last.then_inc(S["gu_ready"], 1)

                            def transposes(q):
                                pe.wait_ge(S["h_ready"], at_(2, g, q + 1))
                                pe.wait_ge(S["hT_ready"], at_(2, g, q))
                                for f in range(2):
                                    last = pe.transpose(bank[3][:, f * P:(f + 1) * P], hh[:, f * P:(f + 1) * P], ident)
                                last.then_inc(S["hT_psum"], 1)

                            def down(q):
                                pe.wait_ge(S["hT_ready"], at_(2, g, q + 1))
                                pe.wait_ge(S["y_low"], at_(2, g, q))
                                for j in range(2):
                                    pe.wait_ge(down_in[2 * q + j].h, down_expected(at_, 2 * q + j, g))
                                for half in range(2):
                                    for f in range(2):
                                        for j in range(2):
                                            s_ = 2 * q + j
                                            o = GUW + D * f + 512 * half
                                            last = pe.matmul(ybank[64 * j:64 * j + 64, half, :], hTs[q][:, f, CAP * j:CAP * j + CAP],
                                                             ring[:, s_, o:o + 512], start=(f == 0), stop=(f == 1))
                                last.then_inc(S["y_psum"], 1)

                            def sums(q):
                                pe.wait_ge(S["y_low"], at_(2, g, q + 1))
                                pe.wait_ge(S["onehotT_ready"], at_(2, g, 2, 1))
                                for m in range(KC):
                                    if q or m >= 2:
                                        pe.wait_ge(S["sum_added"], at_(16, g, 8 * q + m - 1))
                                    for part in range(2):
                                        last = pe.matmul(bank[m % 2][:, 0:T], yst[:, part, m * P:(m + 1) * P], gt[g % 2][:, q, :],
                                                         start=(part == 0), stop=(part == 1))
                                    last.then_inc(S["sum_psum"], 1)

                            gate_up(0)
                            overflow(pe, it, g, 0, dense_of(0))
                            pe.wait_ge(S["sum_added"], at_(16, g, 0))
                            gather_pe(pe, at_, g + 1, (0, 1))
                            transposes(0)
                            gate_up(1)
                            pe.wait_ge(S["hT_ready"], at_(2, g, 1))
                            overflow(pe, it, g, 1, dense_of(0))
                            down(0)
                            transposes(1)
                            gather_pe(pe, at_, g + 1, (2, 3))
                            pe.wait_ge(S["gather_act"], at_(2, g + 1, 2, 1))
                            pe.wait_ge(S["gather_dve"], at_(2, g + 1, 2, 1))
                            sums(0)
                            down(1)
                            onehot_pe(pe, at_, g + 1, e1)
                            sums(1)

                @block.scalar
                def _(act):
                    gather_act(act, zero_at, 0, 0)
                    gather_act(act, zero_at, 0, 2)
                    onehot_act(act, zero_at, 0)
                    with act.Fori(0, PASSES) as it:
                        at_ = At(it)
                        for g in range(GPI):
                            def silu(q):
                                act.wait_ge(S["gu_ready"], at_(2, g, q + 1))
                                act.activation(sg[:, :], bank[2][:, 0:FF], ACT.Silu).then_inc(S["silu_ready"], 1)

                            def h_out(q):
                                act.wait_ge(S["hT_psum"], at_(2, g, q + 1))
                                act.copy(hTs[q][:, :, :], bank[3][:, 0:FF].rearrange("p (f s) -> p f s", s=P)).then_inc(S["hT_ready"], 1)

                            def high(q):
                                act.wait_ge(S["slotw_ready"], at_(1, g, 1, 1))
                                act.wait_ge(S["y_psum"], at_(2, g, q + 1))
                                act.activation(yst[:, 0, :], ybank[:, :, :].rearrange("p a b -> p (a b)"), ACT.Copy,
                                               scale=wsl[g % 2][:, q:q + 1]).then_inc(S["y_high"], 1)

                            silu(0)
                            overflow(act, it, g, 0, dense_of(1))
                            gather_act(act, at_, g + 1, 0)
                            h_out(0)
                            silu(1)
                            overflow(act, it, g, 1, dense_of(1))
                            high(0)
                            h_out(1)
                            gather_act(act, at_, g + 1, 2)
                            high(1)
                            onehot_act(act, at_, g + 1)

                @block.vector
                def _(dve):
                    sel_dve(dve, zero_at, 0, 0)
                    sel_dve(dve, zero_at, 1, 4)
                    gather_dve(dve, zero_at, 0, 1)
                    gather_dve(dve, zero_at, 0, 3)
                    slotw_dve(dve, zero_at, 0)
                    with dve.Fori(0, PASSES) as it:
                        at_ = At(it)
                        for g in range(GPI):
                            def gated(q):
                                dve.wait_ge(S["silu_ready"], at_(2, g, q + 1))
                                dve.tensor_tensor(hh[:, :], sg[:, :], bank[2][:, FF:2 * FF], ALU.mult).then_inc(S["h_ready"], 1)

                            def low(q):
                                dve.wait_ge(S["y_high"], at_(2, g, q + 1))
                                dve.scalar_tensor_tensor(yst[:, 1, :], ybank[:, :, :].rearrange("p a b -> p (a b)"), wsl[g % 2][:, q:q + 1],
                                                         yst[:, 0, :].bitcast(F32), ALU.mult, ALU.subtract).then_inc(S["y_low"], 1)

                            gated(0)
                            dve.wait_ge(S["sum_added"], at_(16, g, 0))
                            overflow(dve, it, g, 0, dense_of(2))
                            gather_dve(dve, at_, g + 1, 1)
                            gated(1)
                            overflow(dve, it, g, 1, dense_of(2))
                            def add_sums(q):
                                for m in range(KC):
                                    if q and m == 0:
                                        dve.wait_ge(S["sum_added"], at_(16, g, 8))
                                    dve.wait_ge(S["sum_psum"], at_(16, g, 8 * q + m + 1))
                                    dve.tensor_tensor(acc[:, m, :], acc[:, m, :], bank[m % 2][:, 0:T], ALU.add).then_inc(S["sum_added"], 1)

                            low(0)
                            gather_dve(dve, at_, g + 1, 3)
                            add_sums(0)
                            low(1)
                            slotw_dve(dve, at_, g + 1)
                            sel_dve(dve, at_, g + 2, it * (4 * GPI) + 4 * (g + 2))
                            add_sums(1)

                @block.vector
                def _(dve):
                    dve.wait_ge(S["sum_added"], (l + 1) * NG * 16 + BASE)
                    for m in range(KC):
                        last = dve.scalar_tensor_tensor(xT[:, m, 0:SEQ], acc[:, m, 0:SEQ], mod[l][:, 40 + m, 0:1], xT[:, m, 0:SEQ], ALU.mult, ALU.add)
                    s_ = sample_view(acc)
                    dve_done.up(dve.tensor_tensor(s_, s_, bc_t(mod[l][:, 40:48, 1:NC_]), ALU.mult))
                    dve_done.wait(dve)
                    dve_done.up(dve.tensor_tensor(xT[:, :, SEQ:T], xT[:, :, SEQ:T], acc[:, :, SEQ:T], ALU.add))
                barrier()

        def gu_expected(at_, s, g):
            return at_.it * 64 + (gu_base[at_layer[0]][s] + 32 * (g + 1))

        def down_expected(at_, s, g):
            return at_.it * 32 + (dn_base[at_layer[0]][s] + 16 * (g + 1))

        at_layer = [0]
        gu_base, dn_base = {}, {}

        def expert_stream(l):
            t_done, y_done = msem("hT_psum"), msem("y_psum")
            used = list(last_item)
            gu_base[l] = [slot_in[s].n for s in range(4)]
            dn_base[l] = [down_in[s].n for s in range(4)]
            wg, wu, wd = a["moe_wg"][l], a["moe_wu"][l], a["moe_wd"][l]
            NG = NE // 4

            @block.sync
            def _(sp):
                def load_gu(s, e):
                    dst = ring[:, s, 0:GUW].rearrange("p (k n) -> p k n", n=512)
                    for w, o in ((wg, 0), (wu, FF)):
                        sp.dma_start(dst[:, :, o:o + FF], w[e].rearrange("(k p) n -> p k n", p=P)).then_inc(slot_in[s].h, 16)

                def load_down(s, e):
                    dst = ring[:, s, GUW:SLOT].rearrange("p (f n) -> p f n", n=D)
                    sp.dma_start(dst, wd[e].rearrange("(f p) n -> p f n", p=P)).then_inc(down_in[s].h, 16)

                for s in range(4):
                    if used[s]:
                        sp.wait_ge(*used[s])
                    load_gu(s, s)
                for s in range(4):
                    if l:
                        sp.wait_ge(y_done, 2 * NG * l + BASE)
                    load_down(s, s)
                with sp.Fori(1, NG) as g:
                    for q in range(2):
                        sp.wait_ge(t_done, g * 2 + (2 * NG * l - 2 + q + 1 + BASE))
                        for j in range(2):
                            load_gu(2 * q + j, sp.snap(g * 4 + (2 * q + j)))
                        sp.wait_ge(y_done, g * 2 + (2 * NG * l - 2 + q + 1 + BASE))
                        for j in range(2):
                            load_down(2 * q + j, sp.snap(g * 4 + (2 * q + j)))
            for s in range(4):
                slot_in[s].n += 32 * NG
                down_in[s].n += 16 * NG
                last_item[s] = (t_done, 2 * NG * (l + 1) + BASE)

        regs_of = {}

        def dense_regs(eng):
            key = str(eng.engine)
            if key not in regs_of:
                r = eng.alloc_register("dense_runs")
                eng.reg_mov(r, 0)
                regs_of[key] = r
            return regs_of[key]

        shared_slots, shared_in, shared_down = {}, {}, {}

        def shared_stream(l, slot):
            @block.sync
            def _(sp):
                if last_item[slot]:
                    sp.wait_ge(*last_item[slot])
                if l:
                    sp.wait_ge(msem("y_psum"), 2 * (NE // 4) * l + BASE)
                dst = ring[:, slot, 0:GUW].rearrange("p (k n) -> p k n", n=512)
                for w, o in ((a["shared_wg"][l], 0), (a["shared_wu"][l], FF)):
                    slot_in[slot].up(sp.dma_start(dst[:, :, o:o + FF], w.rearrange("(k p) n -> p k n", p=P)), 16)
                down_in[slot].up(sp.dma_start(ring[:, slot, GUW:SLOT].rearrange("p (f n) -> p f n", n=D),
                                              a["shared_wd"][l].rearrange("(f p) n -> p f n", p=P)), 16)
            items[0] += 1
            last_item[slot] = (item_used.h, items[0])
            shared_slots[l], shared_in[l], shared_down[l] = slot, slot_in[slot].n, down_in[slot].n

        qkv_slots, qkv_in, win_slots, win_in = [], [], [], []

        def stream_next(parts):
            slot = items[0] % 4
            stream(slot, parts)
            return slot, slot_in[slot].n

        def ada_next(l, r):
            ada_slots[(l, r)], ada_in[(l, r)] = stream_next(columns(a["ada_w"][l], 512 * r))

        def wo_parts(half):
            def parts(dst):
                out = []
                for cp in range(2):
                    for hf in range(2):
                        src = a["swa_wo"][0].rearrange("(kv g d) n -> kv d g n", g=G, d=HD)[2 * cp + hf, :, :, 512 * half:512 * half + 512]
                        out.append((dst[64 * hf:64 * hf + 64, 4 * cp:4 * cp + 4, :], src))
                return out
            return parts

        for r in range(12):
            ada_next(0, r)
        for cch in range(3):
            s_, n_ = stream_next(columns(a["swa_wqkv"][0], 512 * cch))
            qkv_slots.append(s_)
            qkv_in.append(n_)
        for r in range(12):
            ada_next(1, r)
        wo_slots = []
        for half in range(2):
            s_, slot_seen_n = stream_next(wo_parts(half))
            wo_slots.append((s_, slot_seen_n))
        shared_stream(0, items[0] % 4)
        expert_stream(0)
        for cch in range(6):
            s_, n_ = stream_next(columns(a["gla_win"][0], 512 * cch))
            win_slots.append(s_)
            win_in.append(n_)
        gwo_slots = []
        for half in range(2):
            gwo_slots.append(stream_next(columns(a["gla_wo"][0], 512 * half)))
        shared_stream(1, items[0] % 4)
        expert_stream(1)

        @block.gpsimd
        def _(pool):
            for n in LOOP_SEMS:
                pool.sem_inc(msem(n), BASE)

        start()
        swa()
        moe(0)
        gla()
        moe(1)

        norm(vt2[:, V2_FIN:V2_FIN + 8], None)
        with ExitStack() as c:
            yt = sb("yt", [P, 3, D], c=c)
            free = {}
            for n, (t, k4) in enumerate((t, k4) for t in range(3) for k4 in range(2)):
                b = bank[n % 4]
                t0, tn = TILES[t]

                @block.tensor
                def _(pe):
                    act_done.wait(pe)
                    dve_done.wait(pe)
                    for j in range(4):
                        last = pe.transpose(b[0:tn, j * P:(j + 1) * P], hT[:, 4 * k4 + j, t0:t0 + tn], ident)
                    pe_done.up(last)

                @block.vector
                def _(dve):
                    pe_done.wait(dve)
                    dve_done.up(dve.tensor_copy(yt[0:tn, t, 512 * k4:512 * k4 + 512], b[0:tn, :]))

            @block.gpsimd
            def _(pool):
                dve_done.wait(pool)
                stored.up(pool.dma_start(a["y_prompt"][0].rearrange("(t p) d -> p t d", p=P), yt[:, 0:2, :]), 16)
                stored.up(pool.dma_start(a["y_sample"].rearrange("b t d -> (b t) d"), yt[0:NS, 2, :]), 16)
                stored.wait(pool)


_INS = ["x_prompt", "x_sample", "c_prompt", "c_sample", "cache_swa_k", "cache_swa_v", "state_gla",
        "norm_mix_g", "norm_ffn_g", "final_g", "ada_w", "ada_b", "swa_wqkv", "swa_sinks", "swa_wo",
        "gla_win", "gla_wa1", "gla_wa2", "gla_ba", "gla_norm_g", "gla_wo", "moe_router", "moe_bias",
        "moe_wg", "moe_wu", "moe_wd", "shared_wg", "shared_wu", "shared_wd"]
_OUTS = {"y_prompt": (1, SEQ, D), "y_sample": (DB, DT, D),
         "swa_k_prompt": (1, 1, WIN, KVH, HD), "swa_v_prompt": (1, 1, WIN, KVH, HD),
         "swa_k_sample": (1, DB, WIN, KVH, HD), "swa_v_sample": (1, DB, WIN, KVH, HD),
         "gla_state_prompt": (1, 1, GH, DK, DV), "gla_state_sample": (1, DB, GH, DK, DV)}


def kernel(**inputs):
    import concourse.bacc as bacc
    from concourse.bass_utils import run_bass_kernel_spmd

    nc = bacc.Bacc("TRN2", target_bir_lowering=False, num_devices=1)
    arrays = {name: np.ascontiguousarray(inputs[name]) for name in _INS}
    arrays["consts"] = const_table()
    arrays = {f"in_{name}_dram": x for name, x in arrays.items()}
    args = {name[3:-5]: nc.dram_tensor(name, x.shape, mybir.dt.from_np(x.dtype), kind="ExternalInput").ap()
            for name, x in arrays.items()}
    for name, shape in _OUTS.items():
        args[name] = nc.dram_tensor(f"out_{name}_dram", shape, F32, kind="ExternalOutput").ap()
    decoder_step(nc, args)
    r = run_bass_kernel_spmd(nc, [arrays], core_ids=[0])
    return tuple(r.results[0][f"out_{name}_dram"] for name in _OUTS)
```
